# Optimizing a Trainium2 kernel written in Bass

```python
import jax, jax.numpy as jnp
from jax import lax
import numpy as np

D_MODEL = 1024
BATCH = 1
SEQ = 512
DEPTH = 1
DEC_BATCH = 8
DEC_SEQ = 8
PAST_LEN = 2048
PAGE_SIZE = 128

ROPE_THETA = 500000.0
EPS = 1e-6
H_A = 8
HKV_A = 2
DH_A = 64
ROT_A = DH_A // 4
H_IDX = 4
D_IDX = 64
ROT_IDX = D_IDX // 4
TOPK_MAX = 256
H_B = 8
DN_B = 64
DR_B = 32
DV_B = 64
D_CQ = 384
D_C = 256
PEER_HEADS = 8
N_KEYS = 128
N_EXPERTS = N_KEYS * N_KEYS
D_KEY = 128
PEER_TOPK = 16
Q_BLOCK = 128
PEER_BLOCK = 128

IN_WIDTHS = (H_A * DH_A, HKV_A * DH_A, HKV_A * DH_A, H_IDX * D_IDX, D_IDX, H_IDX, D_CQ, D_C, DR_B)
IN_OFFSETS = tuple(sum(IN_WIDTHS[:i + 1]) for i in range(len(IN_WIDTHS) - 1))
D_IN = sum(IN_WIDTHS)
D_MIX = H_A * DH_A + H_B * DV_B

kernel_name = "hymba_dsa_mla_peer_step"

def rms_norm(x, g):
    xf = x.astype(jnp.float32)
    y = xf * lax.rsqrt(jnp.mean(xf * xf, axis=-1, keepdims=True) + EPS)
    return (y * g.astype(jnp.float32)).astype(x.dtype)

def rotary(x, pos, n_rot):
    half = n_rot // 2
    inv = ROPE_THETA ** (-jnp.arange(half, dtype=jnp.float32) * 2.0 / n_rot)
    ang = pos[:, None] * inv[None, :]
    ang = ang.reshape((1, ang.shape[0]) + (1,) * (x.ndim - 3) + (half,))
    cos = jnp.cos(ang).astype(x.dtype)
    sin = jnp.sin(ang).astype(x.dtype)
    x1 = x[..., :half]
    x2 = x[..., half:n_rot]
    return jnp.concatenate([x1 * cos - x2 * sin, x2 * cos + x1 * sin, x[..., n_rot:]], axis=-1)

def mixer_inputs(h, pos, w_in, g_q_a, g_k_a, g_k_idx, g_cq, w_uq, g_ckv, g_q_b):
    n, t, _ = h.shape
    qa, ka, va, qi, ki, wi, cq, ckv, kpe = jnp.split(h @ w_in, IN_OFFSETS, axis=-1)
    qa = rotary(rms_norm(qa.reshape(n, t, H_A, DH_A), g_q_a), pos, ROT_A)
    ka = rotary(rms_norm(ka.reshape(n, t, HKV_A, DH_A), g_k_a), pos, ROT_A)
    va = va.reshape(n, t, HKV_A, DH_A)
    qi = rotary(qi.reshape(n, t, H_IDX, D_IDX), pos, ROT_IDX)
    ki = rotary(rms_norm(ki, g_k_idx), pos, ROT_IDX)
    wi = wi * (H_IDX * D_IDX) ** -0.5
    qb = (rms_norm(cq, g_cq) @ w_uq).reshape(n, t, H_B, DN_B + DR_B)
    qb = rms_norm(jnp.concatenate([qb[..., :DN_B], rotary(qb[..., DN_B:], pos, DR_B)], axis=-1), g_q_b)
    ckv = rms_norm(ckv, g_ckv)
    kpe = rotary(kpe, pos, DR_B)
    return qa, ka, va, qi, ki, wi, qb, ckv, kpe

def mla_keys(ckv, kpe, w_uk, w_uv, g_k_b):
    n, s, _ = ckv.shape
    k_nope = jnp.einsum('nsc,chd->nshd', ckv, w_uk.reshape(D_C, H_B, DN_B))
    k_pe = jnp.broadcast_to(kpe[:, :, None, :], (n, s, H_B, DR_B))
    k = rms_norm(jnp.concatenate([k_nope, k_pe], axis=-1), g_k_b)
    v = jnp.einsum('nsc,chd->nshd', ckv, w_uv.reshape(D_C, H_B, DV_B))
    return k, v

def index_scores(qi, wi, ki):
    s = jax.nn.relu(jnp.einsum('nqhd,nld->nqhl', qi, ki).astype(jnp.float32))
    return jnp.einsum('nqh,nqhl->nql', wi.astype(jnp.float32), s)

def attend_selected(q, k_g, v_g, valid):
    n, t = q.shape[:2]
    qg = q.reshape(n, t, HKV_A, H_A // HKV_A, DH_A)
    s = jnp.einsum('nqhgd,nqkhd->nqhgk', qg, k_g).astype(jnp.float32) * DH_A ** -0.5
    s = jnp.where(valid[:, :, None, None, :], s, -jnp.inf)
    p = jax.nn.softmax(s, axis=-1).astype(v_g.dtype)
    return jnp.einsum('nqhgk,nqkhd->nqhgd', p, v_g).reshape(n, t, H_A * DH_A)

def gather_rows(a, i):
    return jax.vmap(lambda ab, ib: ab[ib])(a, i)

def prompt_mixers(h, proj_w, w_uk, w_uv, g_k_b):
    n, s, _ = h.shape
    pos = jnp.arange(s, dtype=jnp.float32)
    qa, ka, va, qi, ki, wi, qb, ckv, kpe = mixer_inputs(h, pos, *proj_w)
    kb, vb = mla_keys(ckv, kpe, w_uk, w_uv, g_k_b)
    n_blk = s // Q_BLOCK
    k_top = min(TOPK_MAX, s // 4)
    key_pos = jnp.arange(s)
    scale_b = (DN_B + DR_B) ** -0.5

    def to_blocks(a):
        return a.reshape((n, n_blk, Q_BLOCK) + a.shape[2:]).swapaxes(0, 1)

    def block(args):
        qa_b, qi_b, wi_b, qb_b, start = args
        qpos = start + jnp.arange(Q_BLOCK)
        causal = key_pos[None, :] <= qpos[:, None]
        sc = jnp.where(causal[None], index_scores(qi_b, wi_b, ki), -jnp.inf)
        _, idx = lax.top_k(sc, k_top)
        out_a = attend_selected(qa_b, gather_rows(ka, idx), gather_rows(va, idx),
                                idx <= qpos[None, :, None])
        sb = jnp.einsum('nqhd,nshd->nhqs', qb_b, kb).astype(jnp.float32) * scale_b
        pb = jax.nn.softmax(jnp.where(causal[None, None], sb, -jnp.inf), axis=-1).astype(vb.dtype)
        out_b = jnp.einsum('nhqs,nshd->nqhd', pb, vb).reshape(n, Q_BLOCK, H_B * DV_B)
        return jnp.concatenate([out_a, out_b], axis=-1)

    starts = jnp.arange(n_blk) * Q_BLOCK
    o = lax.map(block, (to_blocks(qa), to_blocks(qi), to_blocks(wi), to_blocks(qb), starts))
    o = o.swapaxes(0, 1).reshape(n, s, D_MIX)
    return o, ka, va, ki, ckv, kpe

def sample_mixers(h, cache_a_k, cache_a_v, cache_a_kidx, cache_b_ckv, cache_b_kpe, page_table,
                  proj_w, w_uk, w_uv, g_k_b):
    n, t, _ = h.shape
    n_pages = PAST_LEN // PAGE_SIZE
    L = PAST_LEN + t
    pos = PAST_LEN + jnp.arange(t, dtype=jnp.float32)
    qa, ka, va, qi, ki, wi, qb, ckv, kpe = mixer_inputs(h, pos, *proj_w)
    qpos = PAST_LEN + jnp.arange(t)

    k_top = min(TOPK_MAX, L // 4)
    ki_all = jnp.concatenate([cache_a_kidx[page_table].reshape(n, PAST_LEN, D_IDX), ki], axis=1)
    causal = jnp.arange(L)[None, :] <= qpos[:, None]
    sc = jnp.where(causal[None], index_scores(qi, wi, ki_all), -jnp.inf)
    _, idx = lax.top_k(sc, k_top)
    is_past = (idx < PAST_LEN)[..., None, None]
    phys = jax.vmap(lambda pt, lp: pt[lp])(page_table, jnp.minimum(idx // PAGE_SIZE, n_pages - 1))
    off = idx % PAGE_SIZE
    i_new = jnp.clip(idx - PAST_LEN, 0, t - 1)
    k_g = jnp.where(is_past, cache_a_k[phys, off], gather_rows(ka, i_new))
    v_g = jnp.where(is_past, cache_a_v[phys, off], gather_rows(va, i_new))
    out_a = attend_selected(qa, k_g, v_g, idx <= qpos[None, :, None])

    scale_b = (DN_B + DR_B) ** -0.5

    def page_part(phys_pg):
        k, v = mla_keys(cache_b_ckv[phys_pg], cache_b_kpe[phys_pg], w_uk, w_uv, g_k_b)
        s = jnp.einsum('nqhd,nshd->nhqs', qb, k).astype(jnp.float32) * scale_b
        m = s.max(axis=-1)
        p = jnp.exp(s - m[..., None])
        return m, p.sum(axis=-1), jnp.einsum('nhqs,nshd->nhqd', p, v.astype(jnp.float32))

    m_p, l_p, a_p = lax.map(page_part, page_table.T)
    kb_new, vb_new = mla_keys(ckv, kpe, w_uk, w_uv, g_k_b)
    s_n = jnp.einsum('nqhd,nshd->nhqs', qb, kb_new).astype(jnp.float32) * scale_b
    s_n = jnp.where(jnp.tril(jnp.ones((t, t), dtype=bool))[None, None], s_n, -jnp.inf)
    m_n = s_n.max(axis=-1)
    p_n = jnp.exp(s_n - m_n[..., None])
    l_n = p_n.sum(axis=-1)
    a_n = jnp.einsum('nhqs,nshd->nhqd', p_n, vb_new.astype(jnp.float32))
    m = jnp.maximum(m_p.max(axis=0), m_n)
    c_p = jnp.exp(m_p - m)
    c_n = jnp.exp(m_n - m)
    l_tot = (c_p * l_p).sum(axis=0) + c_n * l_n
    acc = (c_p[..., None] * a_p).sum(axis=0) + c_n[..., None] * a_n
    out_b = (acc / l_tot[..., None]).astype(h.dtype).transpose(0, 2, 1, 3).reshape(n, t, H_B * DV_B)
    return jnp.concatenate([out_a, out_b], axis=-1), ka, va, ki, ckv, kpe

def peer_ffn(h2d, w_peer_q, peer_sub_keys, peer_u, peer_v):
    t = h2d.shape[0]
    nb = -(-t // PEER_BLOCK)
    hp = jnp.pad(h2d, ((0, nb * PEER_BLOCK - t), (0, 0))).reshape(nb, PEER_BLOCK, D_MODEL)

    def block(xb):
        q = (xb @ w_peer_q).reshape(PEER_BLOCK, PEER_HEADS, 2, D_KEY // 2)
        s = jnp.einsum('thpd,hpnd->thpn', q, peer_sub_keys).astype(jnp.float32)
        sv, si = lax.top_k(s, PEER_TOPK)
        cand = (sv[:, :, 0, :, None] + sv[:, :, 1, None, :]).reshape(PEER_BLOCK, PEER_HEADS, PEER_TOPK * PEER_TOPK)
        cv, ci = lax.top_k(cand, PEER_TOPK)
        e = (jnp.take_along_axis(si[:, :, 0], ci // PEER_TOPK, axis=-1) * N_KEYS
             + jnp.take_along_axis(si[:, :, 1], ci % PEER_TOPK, axis=-1))
        g = jax.nn.softmax(cv, axis=-1)
        act = jax.nn.gelu(jnp.einsum('td,thkd->thk', xb, peer_u[e]).astype(jnp.float32))
        return jnp.einsum('thk,thkd->td', (g * act).astype(xb.dtype), peer_v[e])

    return lax.map(block, hp).reshape(nb * PEER_BLOCK, D_MODEL)[:t]

def ffn_residual(x1, g_norm_ffn, w_peer_q, peer_sub_keys, peer_u, peer_v):
    h = rms_norm(x1, g_norm_ffn).reshape(-1, D_MODEL)
    return x1 + peer_ffn(h, w_peer_q, peer_sub_keys, peer_u, peer_v).reshape(x1.shape)

def setup_inputs(seed: int = 0) -> dict:
    key = jax.random.key(seed)
    ks = jax.random.split(key, 32)
    f32 = jnp.float32
    n_pages = PAST_LEN // PAGE_SIZE
    n_used = DEC_BATCH * n_pages
    n_phys = n_used + max(1, n_used // 4)

    def nrm(k, shape, scale=1.0):
        return jax.random.normal(k, shape, f32) * scale

    def gain(k, d):
        return 1.0 + 0.05 * jax.random.normal(k, (d,), f32)

    page_table = jax.random.permutation(ks[7], n_phys)[:n_used].reshape(DEC_BATCH, n_pages).astype(jnp.int32)
    return {
        'x_prompt': nrm(ks[0], (BATCH, SEQ, D_MODEL)),
        'x_sample': nrm(ks[1], (DEC_BATCH, DEC_SEQ, D_MODEL)),
        'cache_a_k': nrm(ks[2], (n_phys, PAGE_SIZE, HKV_A, DH_A)),
        'cache_a_v': nrm(ks[3], (n_phys, PAGE_SIZE, HKV_A, DH_A)),
        'cache_a_kidx': nrm(ks[4], (n_phys, PAGE_SIZE, D_IDX)),
        'cache_b_ckv': nrm(ks[5], (n_phys, PAGE_SIZE, D_C)),
        'cache_b_kpe': nrm(ks[6], (n_phys, PAGE_SIZE, DR_B)),
        'page_table': page_table,
        'g_norm_mix': gain(ks[8], D_MODEL),
        'w_in': nrm(ks[9], (D_MODEL, D_IN), D_MODEL ** -0.5),
        'g_q_a': gain(ks[10], DH_A),
        'g_k_a': gain(ks[11], DH_A),
        'g_k_idx': gain(ks[12], D_IDX),
        'g_cq': gain(ks[13], D_CQ),
        'w_uq': nrm(ks[14], (D_CQ, H_B * (DN_B + DR_B)), D_CQ ** -0.5),
        'g_ckv': gain(ks[15], D_C),
        'w_uk': nrm(ks[16], (D_C, H_B * DN_B), D_C ** -0.5),
        'w_uv': nrm(ks[17], (D_C, H_B * DV_B), D_C ** -0.5),
        'g_q_b': gain(ks[18], DN_B + DR_B),
        'g_k_b': gain(ks[19], DN_B + DR_B),
        'w_out': nrm(ks[20], (D_MIX, D_MODEL), D_MIX ** -0.5),
        'g_norm_ffn': gain(ks[21], D_MODEL),
        'w_peer_q': nrm(ks[22], (D_MODEL, PEER_HEADS * D_KEY), D_MODEL ** -0.5),
        'peer_sub_keys': nrm(ks[23], (PEER_HEADS, 2, N_KEYS, D_KEY // 2), (D_KEY // 2) ** -0.5),
        'peer_u': nrm(ks[24], (N_EXPERTS, D_MODEL), D_MODEL ** -0.5),
        'peer_v': nrm(ks[25], (N_EXPERTS, D_MODEL), PEER_HEADS ** -0.5),
    }

def reference(x_prompt, x_sample, cache_a_k, cache_a_v, cache_a_kidx, cache_b_ckv, cache_b_kpe, page_table,
              g_norm_mix, w_in, g_q_a, g_k_a, g_k_idx, g_cq, w_uq, g_ckv, w_uk, w_uv, g_q_b, g_k_b,
              w_out, g_norm_ffn, w_peer_q, peer_sub_keys, peer_u, peer_v):
    proj_w = (w_in, g_q_a, g_k_a, g_k_idx, g_cq, w_uq, g_ckv, g_q_b)
    yp = x_prompt
    ys = x_sample
    for _ in range(DEPTH):
        o_p, pk, pv, pki, pckv, pkpe = prompt_mixers(rms_norm(yp, g_norm_mix), proj_w, w_uk, w_uv, g_k_b)
        yp = ffn_residual(yp + o_p @ w_out, g_norm_ffn, w_peer_q, peer_sub_keys, peer_u, peer_v)
        o_s, sk, sv, ski, sckv, skpe = sample_mixers(rms_norm(ys, g_norm_mix), cache_a_k, cache_a_v, cache_a_kidx,
                                                     cache_b_ckv, cache_b_kpe, page_table, proj_w, w_uk, w_uv, g_k_b)
        ys = ffn_residual(ys + o_s @ w_out, g_norm_ffn, w_peer_q, peer_sub_keys, peer_u, peer_v)
    return (yp, ys, pk, pv, pki, pckv, pkpe, sk, sv, ski, sckv, skpe)


_drawn_inputs = setup_inputs


def setup_inputs(seed=0):
    import zlib

    import numpy as np

    out = dict(_drawn_inputs(seed))
    spreads = {}
    factors = {'g_q_a': 3.614, 'g_cq': 3.957, 'g_q_b': 4.176, 'g_k_b': 3.906}
    for name, (base, spread) in spreads.items():
        noise = np.random.default_rng([zlib.crc32(name.encode()), seed]).standard_normal(out[name].shape)
        drawn = base * np.exp(spread * noise) if base else spread * noise
        out[name] = __import__('jax').numpy.asarray(drawn.astype(out[name].dtype))
    for name, factor in factors.items():
        out[name] = (out[name] * factor).astype(out[name].dtype)
    return out
```

```python
from contextlib import ExitStack

import concourse.bass as bass
from concourse import mybir

F32 = mybir.dt.float32
I32 = mybir.dt.int32
U32 = mybir.dt.uint32
ALU = mybir.AluOpType
ACT = mybir.ActivationFunctionType
AX = mybir.AxisListType.X
ds = bass.ds

P = 128
D = 1024
SEQ = 512
NB, NT = 8, 8
NTOK = NB * NT
PAST = 2048
PAGE = 128
NPG = PAST // PAGE
NPHYS = 160
HA, KVA, DH = 8, 2, 64
HI, DI = 4, 64
HB, DN, DR, DV = 8, 64, 32, 64
DQK = DN + DR
DCQ, DC = 384, 256
PH, NK, DK, TK = 8, 128, 128, 16
WIDTHS = (HA * DH, KVA * DH, KVA * DH, HI * DI, DI, HI, DCQ, DC, DR)
DIN = sum(WIDTHS)
OQA, OKA, OVA, OQI, OKI, OWI, OCQ, OCKV, OKPE = (sum(WIDTHS[:i]) for i in range(9))
KD = D // P
NTILE = SEQ // P + 1
NCOL = NTILE * P
SAMP = SEQ
EPS = 1e-6
NEG = -1e30
TAKEN = -3e38
G = HA // KVA
KTOP_P = min(256, SEQ // 4)
KTOP_S = min(256, (PAST + NT) // 4)
THETA = 500000.0


def group_cols(n, width=512):
    return [(c, min(width, n - c)) for c in range(0, n, width)]


def program(nc, a, o):
    ctx = ExitStack()
    with ctx:
        def sb(name, shape, dt=F32):
            return ctx.enter_context(nc.sbuf_tensor(name, shape, dt))

        def sem(name):
            return ctx.enter_context(nc.semaphore(name))

        ident = sb("ident", [P, P])
        ones = sb("ones", [P, P])
        rope_a = sb("rope_a", [P, 2, NTILE, 8])
        rope_b = sb("rope_b", [P, 2, NTILE, 16])
        causal = sb("causal", [P, SEQ + 384])
        g_mix_col = sb("g_mix_col", [P, KD])
        g_cq_col = sb("g_cq_col", [P, DCQ // P])
        fold = sb("fold", [P, NTOK])
        new_keys = sb("new_keys", [P, NT])
        new_rows = sb("new_rows", [NTOK, NT])
        pages = sb("pages", [1, NB * NPG], I32)
        stat = sb("stat", [P, 64])
        xall = sb("xall", [P, NTILE, D])
        w_uk = sb("w_uk_s", [P, DC // P, HB * DN])
        w_uv = sb("w_uv_s", [P, DC // P, HB * DV])

        class Region:

            def __init__(self, name, size):
                self.t, self.size, self.at = sb(name, [P, size]), size, 0

            def restart(self, at=0):
                self.at = at

            def view(self, *shape, parts=P, dt=F32):
                n = 1
                for w in shape:
                    n *= w
                x = self.t[0:parts, self.at:self.at + n]
                self.at += n
                assert self.at <= self.size, (self.at, self.size)
                if dt != F32:
                    x = x.bitcast(dt)
                names = "abcd"[:len(shape)]
                if len(shape) > 1:
                    x = x.rearrange(f"p ({' '.join(names)}) -> p {' '.join(names)}", **dict(zip(names, shape)))
                return x

        kept = Region("kept", 18580)
        qaT = kept.view(G, NCOL)
        kaT = kept.view(NCOL)
        qiT = kept.view(2, NCOL)
        kiT = kept.view(NCOL)
        qbT = kept.view(HB, NCOL, parts=DQK)
        kbT = kept.view(HB, NCOL, parts=DQK)
        va = kept.view(NTILE, KVA * DH)
        vb = kept.view(NTILE, HB * DV)
        wi = kept.view(NTILE, HI)

        work = Region("work", 24260)
        w_in = work.view(KD, DIN)
        w_uq = work.view(DCQ // P, HB * DQK)
        cur = work.view(DIN)
        xn_xT = work.at
        xn = work.view(D)
        xT = work.view(KD, P)
        work.restart(xn_xT)
        sq = work.view(DIN)
        work.restart(xn_xT + 2 * D)
        cqT = work.view(DCQ // P, P)
        ckvT = work.view(DC // P, P)
        qb = work.view(HB, DQK)
        kb = work.view(HB, DQK)
        ki2 = work.view(2 * DI)
        rt = work.view(4, 16 * 8)
        g_heads = work.view(HA + KVA, DH)
        g_kidx = work.view(DI)
        g_ckv = work.view(DC)
        g_qk = work.view(2, DQK)
        work.restart()
        oT = work.view(2 * G, NCOL)
        sel_s = work.view(NPG + 1, NTOK)
        w_all = work.view(NB, HI * NT)
        olT = work.view(2, HB, NTOK)
        qabs = work.view(2, HB, NTOK)
        qa_s = work.view(G, NTOK)
        q_pe = work.view(HB, NTOK)
        g_ffn = work.view(D)
        skT = work.view(PH, NK)
        iota16 = work.view(TK)
        AFTER_SEL = work.at
        i_row = work.view((NPG + 1) * P)
        AFTER_ROW = work.at
        w_diag = work.view(HI, NTOK)
        kidx = [work.view(NPG, DI) for _ in range(2)]
        kidxT = work.view(NPG + 1, P)
        w_relu = work.view(NPG + 1, HI * NT)
        i_all = work.view(NPG + 1, NTOK)
        ukT = work.view(4, DC)
        qi_s = work.view(HI, NTOK)
        work.restart(AFTER_ROW)
        sel = work.view(4, SEQ)
        topk = work.view(SEQ)
        relus = work.view(HI, SEQ)
        q_idx = work.view(2, P)
        q_cur = work.view(2, SEQ)
        s_cur = work.view(2, SEQ)
        p_cur = work.view(2, SEQ)
        pT = work.view(2, SEQ)
        o_pair = work.view(4, P)
        work.restart(AFTER_SEL)
        k_s = work.view(NPG + 1, P)
        c_s = work.view(NPG + 1, DC + 1)
        pe_s = work.view(NPG + 1, DR)
        pe_sq = work.view(NPG + 1, DR)
        q_blk = work.view(NTOK)
        kT_s = work.view(2, 4, P)
        cT_s = work.view(2, 3, P)
        sq_s = work.view(2, HB * DN)
        s_s = work.view(NPG + 1, NTOK)
        norm_s = work.view(NPG + 1, HB)
        pe_norm = work.view(NPG + 1)
        m_s = work.view(NTOK)
        m_diag = work.view(NTOK)
        o_s = work.view(DC)
        kept.restart()
        w_out = kept.view(KD, D)
        w_pq = kept.view(KD, D)
        experts = kept.view(NTILE, P, dt=U32)
        gates = kept.view(NTILE, P)
        work.restart(AFTER_SEL)
        o_cur = work.view(KD, P)
        h_row = work.view(D)
        h2T = work.view(KD, P)
        qpT = work.view(PH, P)
        sv = work.view(PH, 2, TK)
        si = work.view(PH, 2, TK, dt=U32)
        sif = work.view(PH, 2, TK)
        sk_at = work.at
        sk = work.view(PH * 2, DK // 2)
        work.restart(sk_at)
        cand = work.view(PH, TK * TK)
        s_pk = work.view(2 * PH, NK)
        cv = work.view(PH, TK)
        ci = work.view(PH, TK, dt=U32)
        ci2 = work.view(PH, TK, dt=U32)
        cif = work.view(2, PH, TK)
        hot = work.view(PH * TK, TK)
        esel = work.view(2, PH, TK)
        m_gate = work.view(PH)
        kept.restart()
        NRING = 8
        EACH = 4
        NDIAG = 4
        ring = kept.view(NRING, D)
        h_cur = kept.view(D)
        e_u = kept.view(P, dt=U32)
        e_v = kept.view(P, dt=U32)
        acts = kept.view(P)
        wts = kept.view(P)
        diag = kept.view(NDIAG, P)
        acc = kept.view(D)
        y_cur = kept.view(D)
        v_s = kept.view(NPG + 1, P + 1)
        assert kept.at <= 2 * KD * D

        ps = [ctx.enter_context(nc.psum_tensor(f"ps{i}", [P, 512], F32)) for i in range(8)]

        const_in = sem("const_in")
        x_in = sem("x_in")
        weights_in = sem("weights_in")
        x_sum = sem("x_sum")
        x_mean = sem("x_mean")
        x_root = sem("x_root")
        x_normed = sem("x_normed")
        x_turned = sem("x_turned")
        xT_ready = sem("xT_ready")
        proj_done = sem("proj_done")
        cur_ready = sem("cur_ready")
        cur_mean = sem("cur_mean")
        cur_root = sem("cur_root")
        cur_normed = sem("cur_normed")
        cur_turned = sem("cur_turned")
        latents_ready = sem("latents_ready")
        up_done = sem("up_done")
        up_ready = sem("up_ready")
        up_mean = sem("up_mean")
        up_root = sem("up_root")
        up_normed = sem("up_normed")
        up_turned = sem("up_turned")
        tile_kept = sem("tile_kept")
        rows_out = sem("rows_out")

        rows_left = sem("rows_left")

        all_here = sem("all_here")
        S = {n: sem(n) for n in (
            "idx_q", "idx_scored", "idx_relu", "idx_summed", "head_q", "scored", "biased", "exped", "p_turned", "pT_ready",
            "attended", "normed_o", "pair_turned", "pair_kept", "head_done", "pool_step", "pool_made", "q_free", "i_free", "pe_past",
            "kidx_sp0", "kidx_sp1", "kidx_pool0", "kidx_pool1", "kidx_free", "w_diag", "w_bcast", "w_ready", "uk_turned", "uk_ready", "q_lat", "qabs_ready", "qi_ready",
            "i_turned", "i_ready", "i_scored", "i_summed", "i_rows", "i_chosen", "i_back", "sel_ready",
            "k_in", "v_in", "c_in", "pe_in", "k_free", "v_free", "c_free", "pe_free", "q_blk", "k_turned", "k_ready", "a_scored",
            "c_turned", "c_ready", "nope", "squared", "b_scored", "b_mean", "b_root", "reduced",
            "f_weights", "o_cur", "mixed", "f_sum", "f_mean", "f_root", "h_row", "h_turned", "h2T", "q_up", "q_kept", "routed", "s_kept",
            "sk_turned", "skT_ready", "f_centered", "f_exped", "s_free", "o_up", "dve_past", "pool_past",
            "e_u", "e_v", "act_past", "dotted", "gelu", "wts", "diag", "v_done", "acc_done", "y_read", "y_ready", "y_out",
            "m_part", "m_turned", "m_diag", "m_all", "centered", "s_exped", "weighted", "o_scaled", "o_turned", "o_kept", "v_lat")}

        landed = [sem(f"landed{r}") for r in range(NRING)]
        freed = [sem(f"freed{r}") for r in range(NRING)]

        block = ctx.enter_context(nc.Block())

        def hold(eng, s, value):
            eng.wait_ge(s, value)

        def meet(eng, k):
            eng.drain()
            eng.sem_inc(all_here, 1)
            eng.wait_ge(all_here, 5 * k)

        def load_index_keys(eng, queue, g0, g1):
            with eng.Fori(0, NB // 2) as bb:
                for e in range(2):
                    hold(eng, S["kidx_free"], 2 * bb + e + 1)
                    for g in range(g0, g1):
                        page = eng.value_load(pages[0:1, ds((2 * bb + e) * NPG + g, 1)], min_val=0, max_val=NPHYS - 1)
                        eng.dma_start(kidx[e][:, g, :], a["cache_a_kidx"][ds(page, 1)].rearrange("a p c -> (a p) c")).then_inc(S[f"kidx_{queue}{e}"], 16)

        def pool_ready(eng, k=1):
            eng.wait_ge(S["pool_step"], k)

        def s_bank(q):
            return ps[2 + q] if q < 2 else ps[5][:, 256:256 + NTOK]

        SOFT = 2

        UNITS = [(blk, c) for blk in range(4) for c in range(2)]
        NFW = 16 * 7
        NCONST = 16 * (15 + HA + KVA)

        @block.sync
        def _(sp):
            sp.dma_start(ident[:], a["c_ident"]).then_inc(const_in, 16)
            sp.dma_start(xall[:, 0:4, :], a["x_prompt"].rearrange("a (t p) d -> p (a t) d", p=P)).then_inc(x_in, 16)
            for half in range(2):
                sp.dma_start(xall[NTOK * half:NTOK * (half + 1), 4, :], a["x_sample"].rearrange("a t d -> (a t) d")).then_inc(x_in, 16)
            sp.dma_start(g_mix_col[:], a["g_norm_mix"].rearrange("(c p) -> p c", p=P), allow_slow_non_contiguous=True).then_inc(const_in, 16)
            sp.dma_start(g_cq_col[:], a["g_cq"].rearrange("(c p) -> p c", p=P), allow_slow_non_contiguous=True).then_inc(const_in, 16)
            sp.dma_start(rope_a[:], a["c_rope_a"]).then_inc(const_in, 16)
            sp.dma_start(rope_b[:], a["c_rope_b"]).then_inc(const_in, 16)
            sp.dma_start(causal[:], a["c_causal"]).then_inc(const_in, 16)

            sp.dma_start(fold[:], a["c_fold"]).then_inc(const_in, 16)
            sp.dma_start(ones[:], a["c_ones"]).then_inc(const_in, 16)
            sp.dma_start(new_keys[:], a["c_new_keys"]).then_inc(const_in, 16)
            sp.dma_start(new_rows[:], a["c_new_rows"]).then_inc(const_in, 16)
            sp.dma_start(pages[:], a["page_table"].rearrange("(o b) g -> o (b g)", o=1)).then_inc(const_in, 16)

            def row(name, n):
                return a[name].rearrange("(o d) -> o d", o=1).broadcast_to([P, n])

            sp.dma_start(g_kidx[:], row("g_k_idx", DI)).then_inc(const_in, 16)
            sp.dma_start(g_ckv[:], row("g_ckv", DC)).then_inc(const_in, 16)
            sp.dma_start(g_qk[:, 0, :], row("g_q_b", DQK)).then_inc(const_in, 16)
            sp.dma_start(g_qk[:, 1, :], row("g_k_b", DQK)).then_inc(const_in, 16)
            for h in range(HA + KVA):
                sp.dma_start(g_heads[:, h, :], row("g_q_a" if h < HA else "g_k_a", DH)).then_inc(const_in, 16)
            def store(t, dst):
                n = P if dst == "p" else NTOK
                for name, c0, w in (("a_k", OKA, 128), ("a_v", OVA, 128), ("a_kidx", OKI, DI), ("b_ckv", OCKV, DC), ("b_kpe", OKPE, DR)):
                    out = o[f"{dst}_{name}"]
                    rows = out[ds(t * P, P), :] if dst == "p" else out
                    sp.dma_start(rows, cur[0:n, c0:c0 + w]).then_inc(rows_out, 16)

            sp.sem_inc(rows_left, 1)
            with sp.Fori(0, NTILE - 1) as t:
                hold(sp, cur_normed, t + 1)
                store(t, "p")
                sp.wait_ge(rows_out, 16 * 5 * (t + 1))
                sp.sem_inc(rows_left, 1)
            sp.wait_ge(cur_normed, NTILE)
            store(0, "s")
            sp.wait_ge(rows_out, 16 * 5 * NTILE)
            meet(sp, 1)
            pool_ready(sp)
            load_index_keys(sp, "sp", 0, NPG // 2)
            meet(sp, 2)
            meet(sp, 3)

            def load_router(again):
                for k in range(KVA):
                    rows = a["w_out"][k * G * DH:(k + 1) * G * DH, :].rearrange("(g d) n -> d g n", g=G)
                    sp.dma_start(w_out[k * DH:(k + 1) * DH, 0:G, :], rows).then_inc(S["f_weights"], 16)
                sp.dma_start(w_out[:, G:, :], a["w_out"][HA * DH:, :].rearrange("(c p) n -> p c n", p=P)).then_inc(S["f_weights"], 16)
                sp.dma_start(w_pq[:], a["w_peer_q"].rearrange("(c p) n -> p c n", p=P)).then_inc(S["f_weights"], 16)
                if not again:
                    sp.dma_start(sk[:], a["peer_sub_keys"].rearrange("h p n d -> n (h p) d")).then_inc(S["f_weights"], 16)
                    sp.dma_start(g_ffn[:], row("g_norm_ffn", D)).then_inc(S["f_weights"], 16)
                    sp.dma_start(iota16[:], a["c_iota16"]).then_inc(S["f_weights"], 16)

            load_router(False)
            meet(sp, 4)
            pool_ready(sp, 3)
            with sp.Fori(0, NB) as b:
                ids = [sp.value_load(pages[0:1, ds(b * NPG + g, 1)], min_val=0, max_val=NPHYS - 1) for g in range(NPG)]
                for key, buf, cache, w, new in (("k", k_s, "cache_a_k", P, "s_a_k"), ("pe", pe_s, "cache_b_kpe", DR, "s_b_kpe"),
                                                ("v", v_s, "cache_a_v", P, "s_a_v"), ("c", c_s, "cache_b_ckv", DC, "s_b_ckv")):
                    hold(sp, S[key + "_free"], b + 1)
                    flat = a[cache].rearrange("a p h d -> a p (h d)") if key in "kv" else a[cache]
                    for g in range(NPG):
                        sp.dma_start(buf[:, g, 0:w], flat[ds(ids[g], 1)].rearrange("a p c -> (a p) c")).then_inc(S[key + "_in"], 16)
                    sp.dma_start(buf[0:NT, NPG, 0:w], o[new][ds(b * NT, NT), :]).then_inc(S[key + "_in"], 16)
            meet(sp, 5)
            load_router(True)
            meet(sp, 6)

        @block.gpsimd
        def _(pool):
            meet(pool, 1)
            nc.gpsimd.memset(kidxT[:, NPG, :], 0.0)
            nc.gpsimd.memset(i_row[0:NTOK, PAST:], NEG).then_inc(S["pool_step"], 1)
            load_index_keys(pool, "pool", NPG // 2, NPG)
            meet(pool, 2)
            meet(pool, 3)
            nc.gpsimd.memset(experts[:, NTILE - 1, :], 0).then_inc(S["pool_step"], 1)
            meet(pool, 4)
            for buf in (k_s, v_s, c_s, pe_s):
                nc.gpsimd.memset(buf[:, NPG, :], 0.0)
            nc.gpsimd.memset(q_blk[:], 0.0).then_inc(S["pool_made"], 1)
            pool.wait_ge(S["pool_made"], 1)
            nc.gpsimd.memset(v_s[:, :, P:P + 1], 1.0)
            nc.gpsimd.memset(c_s[:, :, DC:DC + 1], 1.0).then_inc(S["pool_step"], 1)

            def gather(t, cols, eye, width, more=0):
                def weigh(m):
                    if m == 0:
                        hold(pool, S["wts"], t + 1)
                        pool.sem_inc(S["pool_past"], 1)
                    nc.gpsimd.tensor_scalar(diag[:, m // EACH % NDIAG, 0:width], eye, wts[:, m:m + 1], None, ALU.mult).then_inc(S["diag"], 1)

                for k in range(2 * cols):
                    n, r = k % cols, k % NRING
                    if n == 0:
                        hold(pool, S["e_u"] if k == 0 else S["e_v"], t + 1 + (more if k == 0 else 0))
                        pool.sem_inc(S["pool_past"], 1)
                    hold(pool, freed[r], 32 * t + k // NRING + 1)
                    pool.sem_inc(S["pool_past"], 1)
                    table, ids = ("peer_u", e_u) if k < cols else ("peer_v", e_v)
                    pool.indirect_dma_start(ring[:, r, :], None, a[table], bass.IndirectOffsetOnAxis(ap=ids[:, n:n + 1], axis=0)).then_inc(landed[r], 16)
                    if k >= cols + 4 and n % EACH == 0:
                        weigh(n - 4)
                weigh(cols - 4)

            with pool.Fori(0, NTILE - 1) as t:
                gather(t, P, ident[:], P)
            meet(pool, 5)
            meet(pool, 6)
            gather(NTILE - 1, P // 2, fold[:], NTOK, 1)

        @block.scalar
        def _(act):
            act.dma_start(w_in[:], a["w_in"].rearrange("(c p) n -> p c n", p=P)).then_inc(weights_in, 16)
            act.dma_start(w_uq[:], a["w_uq"].rearrange("(c p) n -> p c n", p=P)).then_inc(weights_in, 16)
            act.dma_start(w_uk[:], a["w_uk"].rearrange("(c p) n -> p c n", p=P)).then_inc(weights_in, 16)
            act.dma_start(w_uv[:], a["w_uv"].rearrange("(c p) n -> p c n", p=P)).then_inc(weights_in, 16)
            act.wait_ge(x_in, 48)
            act.wait_ge(const_in, NCONST)
            with act.Fori(0, NTILE) as t:
                cols = ds(t * P, P)
                hold(act, tile_kept, t + 1)
                nc.scalar.activation(sq[:, 0:D], xall[:, ds(t, 1), :].rearrange("p a d -> p (a d)"), ACT.Square,
                                     accum_out=stat[:, 0:1]).then_inc(x_sum, 1)
                hold(act, x_mean, t + 1)
                nc.scalar.activation(stat[:, 2:3], stat[:, 1:2], ACT.Sqrt).then_inc(x_root, 1)
                hold(act, x_turned, t + 1)
                for c in range(KD):
                    last = nc.scalar.activation(xT[:, c, :], ps[c // 4][:, (c % 4) * P:(c % 4 + 1) * P], ACT.Copy,
                                                scale=g_mix_col[:, c:c + 1])
                last.then_inc(xT_ready, 1)
                hold(act, rows_left, t + 1)
                for i, (c0, w) in enumerate(group_cols(DIN)):
                    hold(act, proj_done, 4 * t + i + 1)
                    src, dst = ps[2 + i][:, 0:w], cur[:, c0:c0 + w]
                    if i == 0:
                        src = src.rearrange("p (k g d) -> p k g d", k=KVA, g=G)
                        dst = dst.rearrange("p (g k d) -> p k g d", k=KVA, g=G)
                    last = nc.scalar.activation(dst, src, ACT.Copy)
                last.then_inc(cur_ready, 1)
                hold(act, cur_mean, t + 1)
                nc.scalar.activation(stat[:, 16:29], stat[:, 16:29], ACT.Sqrt).then_inc(cur_root, 1)
                hold(act, cur_turned, t + 1)
                for c in range(3):
                    nc.scalar.activation(cqT[:, c, :], ps[1][:, P + c * P:2 * P + c * P], ACT.Copy, scale=g_cq_col[:, c:c + 1])
                nc.scalar.activation(ckvT[:], ps[6][:, 0:2 * P].rearrange("p (c k) -> p c k", c=2), ACT.Copy).then_inc(latents_ready, 1)
                nc.scalar.activation(qaT[:, :, cols], ps[0][:].rearrange("p (g k) -> p g k", g=G), ACT.Copy)
                nc.scalar.activation(kaT[:, cols], ps[1][:, 0:P], ACT.Copy)
                nc.scalar.activation(kiT[:, cols], ps[6][:, 2 * P:3 * P], ACT.Copy)
                nc.scalar.activation(qiT[:, :, cols], ps[7][:, 0:2 * P].rearrange("p (g k) -> p g k", g=2), ACT.Copy)
                nc.scalar.activation(va[:, ds(t, 1), :], cur[:, OVA:OVA + 128].unsqueeze(1), ACT.Copy)
                nc.scalar.activation(wi[:, ds(t, 1), :], cur[:, OWI:OWI + HI].unsqueeze(1), ACT.Copy)
                hold(act, up_done, t + 1)
                qb2 = qb[:].rearrange("p h d -> p (h d)")
                nc.scalar.activation(qb2[:, 0:512], ps[2][:], ACT.Copy)
                nc.scalar.activation(qb2[:, 512:768], ps[3][:, 0:256], ACT.Copy)
                nc.scalar.activation(kb[:, :, 0:DN], ps[4][:].rearrange("p (h d) -> p h d", h=HB), ACT.Copy)
                nc.scalar.activation(vb[:, ds(t, 1), :], ps[5][:].unsqueeze(1), ACT.Copy).then_inc(up_ready, 1)
                hold(act, up_mean, t + 1)
                nc.scalar.activation(stat[:, 32:48], stat[:, 32:48], ACT.Sqrt).then_inc(up_root, 1)
                hold(act, up_turned, t + 1)
                for i in range(2):
                    nc.scalar.activation(qbT[:, 4 * i:4 * i + 4, cols], ps[i][0:DQK, :].rearrange("p (g k) -> p g k", g=4), ACT.Copy)
                    last = nc.scalar.activation(kbT[:, 4 * i:4 * i + 4, cols], ps[2 + i][0:DQK, :].rearrange("p (g k) -> p g k", g=4), ACT.Copy)
                last.then_inc(tile_kept, 1)
            meet(act, 1)
            for h in range(HI):
                nc.scalar.activation(qi_s[0:DI, h, :], qiT[64 * (h % 2):64 * (h % 2) + 64, h // 2, SAMP:SAMP + NTOK], ACT.Copy)
            nc.scalar.activation(q_pe[0:DR], qbT[DN:DQK, :, SAMP:SAMP + NTOK], ACT.Copy).then_inc(S["qi_ready"], 1)
            act.wait_ge(S["w_bcast"], 1)
            nc.scalar.activation(w_all[:].rearrange("p b (h t) -> p b h t", h=HI), ps[6][:, 0:HI * NTOK].rearrange("p (h b t) -> p b h t", h=HI, b=NB), ACT.Copy).then_inc(S["w_ready"], 1)
            for i in range(2):
                act.wait_ge(S["uk_turned"], i + 1)
                for j in range(2):
                    last = nc.scalar.activation(ukT[0:DN, 2 * j:2 * j + 2, :], ps[j][0:DN, :].rearrange("p (h c) -> p h c", h=2), ACT.Copy)
                last.then_inc(S["uk_ready"], 1)
                act.wait_ge(S["q_lat"], i + 1)
                nc.scalar.activation(qabs[:, :, 4 * i:4 * i + 4, :].rearrange("p c h t -> p h c t"),
                                     ps[2 + i][:].rearrange("p (h c t) -> p h c t", h=4, c=2), ACT.Copy).then_inc(S["qabs_ready"], 1)
            pool_ready(act)
            with act.Fori(0, NB // 2) as bb:
                for e in range(2):
                    b = 2 * bb + e
                    hold(act, S["i_turned"], b + 1)
                    nc.scalar.activation(kidxT[0:DI, NPG, 0:NT], kiT[0:DI, ds(SAMP + b * NT, NT)], ACT.Copy)
                    for q in range(4):
                        last = nc.scalar.activation(kidxT[0:DI, 4 * q:4 * q + 4, :], ps[q][0:DI, :].rearrange("p (g k) -> p g k", g=4), ACT.Copy)
                    last.then_inc(S["i_ready"], 1)
            meet(act, 2)
            with act.Fori(0, 4) as i:
                hold(act, S["idx_summed"], i + 1)
                nc.scalar.activation(q_idx[:], qiT[:, :, ds(i * P, P)], ACT.Copy).then_inc(S["idx_q"], 1)
                for h in range(HI):
                    hold(act, S["idx_scored"], HI * i + h + 1)
                    nc.scalar.activation(relus[:, h, :], ps[h][:], ACT.Relu).then_inc(S["idx_relu"], 1)

            def attention(first, q_src, k_scale, o_chunk):
                with act.Fori(0, 4) as g:
                    n0 = first + 8 * g
                    hold(act, S["head_done"], g + 1 + first // 8)
                    q_src(g).then_inc(S["head_q"], 1)
                    for u, (blk, c) in enumerate(UNITS):
                        nk = (blk + 1) * P
                        hold(act, S["biased"], n0 + u + 1)
                        nc.scalar.activation(p_cur[:, u % 2, 0:nk], s_cur[:, u % 2, 0:nk], ACT.Exp, scale=k_scale,
                                             bias=stat[:, 2 + u % 2:3 + u % 2],
                                             accum_out=stat[:, 4 + u % 2:5 + u % 2]).then_inc(S["exped"], 1)
                        hold(act, S["p_turned"], n0 + u + 1)
                        nc.scalar.activation(pT[:, u % 2, 0:nk], ps[2 + u % 2][:, 0:nk], ACT.Copy).then_inc(S["pT_ready"], 1)
                    hold(act, S["pair_turned"], g + 1 + first // 8)
                    nc.scalar.activation(oT[:, ds(g + o_chunk, 1), 0:SEQ], ps[6][:].unsqueeze(1), ACT.Copy).then_inc(S["pair_kept"], 1)

            attention(0, lambda g: nc.scalar.activation(q_cur[:, 0:1, :], qaT[:, ds(g, 1), 0:SEQ], ACT.Copy), DH ** -0.5, 0)
            attention(32, lambda g: nc.scalar.activation(q_cur[0:DQK, :, :], qbT[:, ds(2 * g, 2), 0:SEQ], ACT.Copy), DQK ** -0.5, G)
            act.wait_ge(S["i_back"], 1)
            for q, (g0, n) in enumerate(group_cols(NPG + 1, 8)):
                nc.scalar.activation(sel_s[:, g0:g0 + n, :], ps[q][:, 0:n * NTOK].rearrange("p (g t) -> p g t", g=n), ACT.Copy)
            nc.scalar.activation(qa_s[:], qaT[:, :, SAMP:SAMP + NTOK], ACT.Copy)
            meet(act, 3)
            act.wait_ge(S["sk_turned"], 1)
            for j in range(2):
                last = nc.scalar.activation(skT[:, 4 * j:4 * j + 4, :], ps[j][:].rearrange("p (h n) -> p h n", h=4), ACT.Copy)
            last.then_inc(S["skT_ready"], 1)

            def route(t):
                nc.scalar.activation(o_cur[:], oT[:, :, ds(t * P, P)], ACT.Copy).then_inc(S["o_cur"], 1)
                hold(act, S["mixed"], 2 * t + 2)
                x1 = xall[:, ds(t, 1), :].rearrange("p a d -> p (a d)")
                nc.scalar.activation(h_row[:], x1, ACT.Square, accum_out=stat[:, 40:41]).then_inc(S["f_sum"], 1)
                hold(act, S["f_mean"], t + 1)
                nc.scalar.activation(stat[:, 42:43], stat[:, 41:42], ACT.Sqrt).then_inc(S["f_root"], 1)
                hold(act, S["h_row"], t + 1)
                act.sem_inc(S["act_past"], 1)
                nc.scalar.activation(oT[:, :, ds(t * P, P)], h_row[:].rearrange("p (c k) -> p c k", c=KD), ACT.Copy)
                hold(act, S["h_turned"], t + 1)
                for j in range(2):
                    last = nc.scalar.activation(h2T[:, 4 * j:4 * j + 4, :], ps[2 + j][:].rearrange("p (c k) -> p c k", c=4), ACT.Copy)
                last.then_inc(S["h2T"], 1)
                for j in range(2):
                    hold(act, S["q_up"], 2 * t + j + 1)
                    nc.scalar.activation(qpT[:, 4 * j:4 * j + 4, :], ps[4 + j][:].rearrange("p (h k) -> p h k", h=4), ACT.Copy).then_inc(S["q_kept"], 1)
                hold(act, S["s_free"], t + 1)
                for j, bank in enumerate((0, 1, 6, 7)):
                    hold(act, S["routed"], 4 * t + j + 1)
                    nc.scalar.activation(s_pk[:, 4 * j:4 * j + 4, :], ps[bank][:].rearrange("p (h k) -> p h k", h=4), ACT.Copy).then_inc(S["s_kept"], 1)

            def gate(t):
                hold(act, S["f_centered"], t + 1)
                nc.scalar.activation(cv[:], cv[:], ACT.Exp).then_inc(S["f_exped"], 1)

            route(0)
            with act.Fori(0, NTILE - 2) as t:
                route(t + 1)
                gate(t)
            gate(NTILE - 2)
            meet(act, 4)
            pool_ready(act, 3)

            def softmax(n, scale):
                hold(act, S["centered"], n)
                nc.scalar.activation(s_s[:], s_s[:], ACT.Exp, scale=scale).then_inc(S["s_exped"], 1)

            def sample_attention(b):
                cols = ds(SAMP + b * NT, NT)
                hold(act, S["q_free"], b + 1)
                for c in range(KVA):
                    r = slice(64 * c, 64 * c + 64)
                    last = nc.scalar.activation(q_blk[r, 32 * c:32 * c + 32].rearrange("p (g t) -> p g t", g=G), qa_s[r, :, ds(b * NT, NT)], ACT.Copy)
                last.then_inc(S["q_blk"], 1)
                for q, (g0, n) in enumerate(group_cols(NPG + 1, 4)):
                    hold(act, S["k_turned"], 5 * b + q + 1)
                    nc.scalar.activation(kT_s[:, q % 2, 0:n, :], ps[q % 2][:, 0:n * P].rearrange("p (g k) -> p g k", g=n), ACT.Copy).then_inc(S["k_ready"], 1)
                softmax(SOFT * b + 1, DH ** -0.5)
                hold(act, S["o_turned"], SOFT * b + 1)
                for c in range(KVA):
                    r = slice(64 * c, 64 * c + 64)
                    last = nc.scalar.activation(oT[r, 0:G, cols], ps[5][r, 32 * c:32 * c + 32].rearrange("p (g t) -> p g t", g=G), ACT.Copy)
                last.then_inc(S["o_kept"], 1)
                for g in range(NPG + 1):
                    n = (NPG + 1) * b + g + 1
                    hold(act, S["c_turned"], n)
                    nc.scalar.activation(cT_s[:, g % 2, 0:2, :], ps[g % 2][:, 0:2 * P].rearrange("p (c k) -> p c k", c=2), ACT.Copy)
                    nc.scalar.activation(cT_s[0:DR, g % 2, 2, :], ps[g % 2][0:DR, 2 * P:3 * P], ACT.Copy).then_inc(S["c_ready"], 1)
                    hold(act, S["nope"], n)
                    if g >= 2:
                        hold(act, S["reduced"], n - 2)
                    nc.scalar.activation(sq_s[:, g % 2, :], ps[4][:], ACT.Square).then_inc(S["squared"], 1)
                hold(act, S["b_mean"], b + 1)
                nc.scalar.activation(norm_s[:], norm_s[:], ACT.Sqrt).then_inc(S["b_root"], 1)
                softmax(SOFT * b + 2, DQK ** -0.5)
                hold(act, S["o_turned"], SOFT * b + 2)
                nc.scalar.activation(olT[:, :, :, ds(b * NT, NT)].rearrange("p c h t -> p (c h) t"),
                                     ps[5][:, 0:2 * NTOK].rearrange("p (x t) -> p x t", t=NT), ACT.Copy).then_inc(S["o_kept"], 1)

            def gelu(t, cols):
                hold(act, S["dotted"], t + 1)
                nc.scalar.activation(acts[:, 0:cols], acts[:, 0:cols], ACT.Gelu_apprx_tanh).then_inc(S["gelu"], 1)

            act.sem_inc(S["y_out"], 16)
            with act.Fori(0, NTILE - 1) as t:
                sample_attention(2 * t)
                gelu(t, P)
                sample_attention(2 * t + 1)
                hold(act, S["y_ready"], t + 1)
                act.dma_start(o["p_y"][ds(t * P, P), :], y_cur[:]).then_inc(S["y_out"], 16)
            act.wait_ge(S["v_lat"], 1)
            for j in range(4):
                for c in range(2):
                    r = slice(64 * c, 64 * c + 64)
                    nc.scalar.activation(oT[r, G + j, SAMP:SAMP + NTOK], ps[0][r, P * j + 64 * c:P * j + 64 * c + 64], ACT.Copy)
            act.drain()
            nc.scalar.activation(oT[:, :, SAMP + NTOK:SAMP + 2 * NTOK], oT[:, :, SAMP:SAMP + NTOK], ACT.Copy)
            act.wait_ge(S["y_out"], 16 * NTILE)
            meet(act, 5)
            route(NTILE - 1)
            gate(NTILE - 1)
            meet(act, 6)
            gelu(NTILE - 1, P // 2)
            act.wait_ge(S["y_ready"], NTILE)
            act.dma_start(o["s_y"], y_cur[0:NTOK]).then_inc(S["y_out"], 16)
            act.wait_ge(S["y_out"], 16 * (NTILE + 1))

        @block.vector
        def _(dve):
            v = nc.vector

            def settle():
                dve.drain()

            def rope(x, n, half, tab, t, at):
                shape = [P, n, half]
                cos = tab[:, 0, ds(t, 1), :].broadcast_to(shape)
                sin = tab[:, 1, ds(t, 1), :].broadcast_to(shape)
                x1, x2 = x[:, :, 0:half], x[:, :, half:2 * half]
                tmp = [rt[:, i, 0:n * half].rearrange("p (n k) -> p n k", n=n) for i in range(4)]
                v.tensor_tensor(tmp[0], x1, cos, ALU.mult)
                v.tensor_tensor(tmp[1], x2, sin, ALU.mult)
                v.tensor_tensor(tmp[2], x2, cos, ALU.mult)
                v.tensor_tensor(tmp[3], x1, sin, ALU.mult)
                settle()
                v.tensor_tensor(x1, tmp[0], tmp[1], ALU.subtract)
                v.tensor_tensor(x2, tmp[2], tmp[3], ALU.add)
                settle()

            dve.wait_ge(const_in, NCONST)
            dve.wait_ge(x_in, 48)
            v.tensor_tensor(g_qk[:, 0, :], g_qk[:, 0, :], g_qk[:, 1, :], ALU.mult).then_inc(tile_kept, 1)
            with dve.Fori(0, NTILE) as t:
                hold(dve, x_sum, t + 1)
                v.tensor_scalar(stat[:, 1:2], stat[:, 0:1], 1.0 / D, EPS, ALU.mult, ALU.add).then_inc(x_mean, 1)
                hold(dve, x_root, t + 1)
                v.reciprocal(stat[:, 3:4], stat[:, 2:3])
                settle()
                v.tensor_scalar(xn[:], xall[:, ds(t, 1), :].rearrange("p a d -> p (a d)"), stat[:, 3:4], None,
                                ALU.mult).then_inc(x_normed, 1)
                hold(dve, cur_ready, t + 1)
                v.tensor_tensor(sq[:], cur[:], cur[:], ALU.mult)
                settle()
                v.tensor_reduce(stat[:, 16:26], sq[:, 0:640].rearrange("p (h d) -> p h d", d=DH), AX, ALU.add)
                v.tensor_reduce(stat[:, 26:27], sq[:, OKI:OKI + DI], AX, ALU.add)
                v.tensor_reduce(stat[:, 27:28], sq[:, OCQ:OCQ + DCQ], AX, ALU.add)
                v.tensor_reduce(stat[:, 28:29], sq[:, OCKV:OCKV + DC], AX, ALU.add)
                settle()
                v.tensor_scalar(stat[:, 16:27], stat[:, 16:27], 1.0 / DH, EPS, ALU.mult, ALU.add)
                v.tensor_scalar(stat[:, 27:28], stat[:, 27:28], 1.0 / DCQ, EPS, ALU.mult, ALU.add)
                v.tensor_scalar(stat[:, 28:29], stat[:, 28:29], 1.0 / DC, EPS, ALU.mult, ALU.add).then_inc(cur_mean, 1)
                hold(dve, cur_root, t + 1)
                v.reciprocal(stat[:, 16:29], stat[:, 16:29])
                settle()
                heads = cur[:, 0:640].rearrange("p (h d) -> p h d", d=DH)
                v.tensor_tensor(heads, heads, stat[:, 16:26].unsqueeze(2).broadcast_to([P, 10, DH]), ALU.mult)
                v.tensor_scalar(cur[:, OCQ:OCQ + DCQ], cur[:, OCQ:OCQ + DCQ], stat[:, 27:28], None, ALU.mult)
                ki, ckv = cur[:, OKI:OKI + DI], cur[:, OCKV:OCKV + DC]
                v.scalar_tensor_tensor(ki, ki, stat[:, 26:27], g_kidx[:], ALU.mult, ALU.mult)
                v.scalar_tensor_tensor(ckv, ckv, stat[:, 28:29], g_ckv[:], ALU.mult, ALU.mult)
                settle()
                v.tensor_tensor(heads, heads, g_heads[:], ALU.mult)
                settle()
                rope(heads, 10, 8, rope_a, t, 0)
                rope(cur[:, OQI:OQI + 320].rearrange("p (h d) -> p h d", d=DI), 5, 8, rope_a, t, 0)
                rope(cur[:, OKPE:OKPE + DR].unsqueeze(1), 1, 16, rope_b, t, 0)
                v.tensor_copy(ki2[:].rearrange("p (a d) -> p a d", a=2), cur[:, OKI:OKI + DI].unsqueeze(1).broadcast_to([P, 2, DI]))
                v.tensor_copy(kb[:, :, DN:DQK], cur[:, OKPE:OKPE + DR].unsqueeze(1).broadcast_to([P, HB, DR])).then_inc(cur_normed, 1)
                hold(dve, up_ready, t + 1)
                rope(qb[:, :, DN:DQK], HB, 16, rope_b, t, 0)
                s8 = sq[:, 0:768].rearrange("p (h d) -> p h d", d=DQK)
                s8b = sq[:, 768:1536].rearrange("p (h d) -> p h d", d=DQK)
                v.tensor_tensor(s8, qb[:], qb[:], ALU.mult)
                v.tensor_tensor(s8b, kb[:], kb[:], ALU.mult)
                settle()
                v.tensor_reduce(stat[:, 32:48], sq[:, 0:1536].rearrange("p (h d) -> p h d", d=DQK), AX, ALU.add)
                settle()
                v.tensor_scalar(stat[:, 32:48], stat[:, 32:48], 1.0 / DQK, EPS, ALU.mult, ALU.add).then_inc(up_mean, 1)
                hold(dve, up_root, t + 1)
                v.reciprocal(stat[:, 32:48], stat[:, 32:48])
                settle()
                v.tensor_tensor(kb[:], kb[:], stat[:, 40:48].unsqueeze(2).broadcast_to([P, HB, DQK]), ALU.mult)
                v.tensor_tensor(qb[:], qb[:], stat[:, 32:40].unsqueeze(2).broadcast_to([P, HB, DQK]), ALU.mult)
                settle()
                v.tensor_tensor(qb[:], qb[:], g_qk[:, 0:1, :].broadcast_to([P, HB, DQK]), ALU.mult).then_inc(up_normed, 1)
            meet(dve, 1)
            for h in range(HI):
                last = v.tensor_scalar(w_diag[0:NTOK, h, :], ident[0:NTOK, 0:NTOK], wi[0:NTOK, 4, h:h + 1], (HI * DI) ** -0.5, ALU.mult, ALU.mult)
            last.then_inc(S["w_diag"], 1)
            dve.wait_ge(S["w_ready"], 1)
            dve.sem_inc(S["i_free"], 1)
            with dve.Fori(0, NB) as b:
                hold(dve, S["i_scored"], b + 1)
                w = w_all[:, ds(b, 1), :]
                for bank, g0, n in ((4, 0, NPG), (5, NPG, 1)):
                    v.scalar_tensor_tensor(w_relu[:, g0:g0 + n, :], ps[bank][:, 0:n * 32].rearrange("p (g x) -> p g x", g=n),
                                           0.0, w.broadcast_to([P, n, HI * NT]), ALU.max, ALU.mult)
                settle()
                dve.sem_inc(S["i_free"], 1)
                v.tensor_reduce(i_all[:, :, ds(b * NT, NT)], w_relu[:].rearrange("p g (h t) -> p g t h", h=HI), AX, ALU.add)
                settle()
            dve.sem_inc(S["i_summed"], 1)
            dve.wait_ge(S["i_rows"], 1)
            pool_ready(dve)
            for q in range(4):
                v.tensor_copy(i_row[0:NTOK, 512 * q:512 * q + 512], ps[q][0:NTOK, :])
            v.tensor_tensor(i_row[0:NTOK, PAST:PAST + NT], ps[5][0:NTOK, 0:NT], new_rows[:], ALU.add)
            settle()
            meet(dve, 2)
            dve.sem_inc(S["idx_summed"], 1)
            with dve.Fori(0, 4) as i:
                for h in range(HI):
                    hold(dve, S["idx_relu"], HI * i + h + 1)
                    w = wi[:, ds(i, 1), h:h + 1].rearrange("p a b -> p (a b)")
                    seen = causal[:, ds(384 - i * P, SEQ)]
                    v.scalar_tensor_tensor(topk[:], relus[:, h, :], w, seen if h == 0 else topk[:], ALU.mult, ALU.add)
                    settle()
                dve.sem_inc(S["idx_summed"], 1)
                for r in range(KTOP_P // 8):
                    v.max(stat[:, 8:16], topk[:])
                    settle()
                    v.match_replace(topk[:], stat[:, 8:16], topk[:], TAKEN)
                    settle()
                v.tensor_scalar(topk[:], topk[:], TAKEN, -NEG, ALU.is_equal, ALU.mult)
                settle()
                v.scalar_tensor_tensor(sel[:, ds(i, 1), :], topk[:].unsqueeze(1), NEG, causal[:, ds(384 - i * P, SEQ)].unsqueeze(1), ALU.add, ALU.add)
                settle()
            dve.sem_inc(S["head_done"], 1)

            scores = i_row[0:NTOK, 0:PAST + NT]
            assert KTOP_S // 8 * 2 == 8 * len(UNITS)

            def choose(u):
                if u % 2 == 0:
                    v.max(stat[0:NTOK, 24:32], scores)
                else:
                    v.match_replace(scores, stat[0:NTOK, 24:32], scores, TAKEN)
                settle()

            def attention(first, scale, mask):
                with dve.Fori(0, 4) as g:
                    n0 = first + 8 * g

                    def out(u):
                        blk, c = UNITS[u]
                        hold(dve, S["attended"], n0 + u + 1)
                        v.reciprocal(stat[:, 6:7], stat[:, 4 + u % 2:5 + u % 2])
                        settle()
                        v.tensor_scalar(o_pair[:, blk, c * 64:c * 64 + 64], ps[4 + u % 2][:, 0:64], stat[:, 6:7], None,
                                        ALU.mult).then_inc(S["normed_o"], 1)
                        settle()

                    for u, (blk, c) in enumerate(UNITS):
                        nk = (blk + 1) * P
                        hold(dve, S["scored"], n0 + u + 1)
                        v.tensor_tensor(s_cur[:, u % 2, 0:nk], ps[u % 2][:, 0:nk], mask(blk, nk), ALU.add)
                        settle()
                        v.tensor_reduce(stat[:, 7:8], s_cur[:, u % 2, 0:nk], AX, ALU.max)
                        settle()
                        v.tensor_scalar(stat[:, 2 + u % 2:3 + u % 2], stat[:, 7:8], -scale, None, ALU.mult).then_inc(S["biased"], 1)
                        choose(u)
                        if u:
                            out(u - 1)
                    out(7)

            attention(0, DH ** -0.5, lambda blk, nk: sel[:, blk, 0:nk])
            attention(32, DQK ** -0.5, lambda blk, nk: causal[:, 384 - blk * P:384 - blk * P + nk])
            v.tensor_scalar(scores, scores, TAKEN, -NEG, ALU.is_equal, ALU.mult)
            settle()
            v.tensor_scalar(scores, scores, NEG, None, ALU.add)
            settle()
            v.tensor_tensor(i_row[0:NTOK, PAST:PAST + NT], i_row[0:NTOK, PAST:PAST + NT], new_rows[:], ALU.add).then_inc(S["i_chosen"], 1)
            meet(dve, 3)
            dve.wait_ge(S["f_weights"], NFW)
            pool_ready(dve, 2)
            dve.sem_inc(S["s_free"], 1)

            def mix(t):
                for j in range(2):
                    hold(dve, S["o_up"], 2 * t + j + 1)
                    x1 = xall[:, ds(t, 1), 512 * j:512 * j + 512].rearrange("p a d -> p (a d)")
                    v.tensor_tensor(x1, x1, ps[j][:], ALU.add).then_inc(S["mixed"], 1)
                yield
                hold(dve, S["f_sum"], t + 1)
                v.tensor_scalar(stat[:, 41:42], stat[:, 40:41], 1.0 / D, EPS, ALU.mult, ALU.add).then_inc(S["f_mean"], 1)
                yield
                hold(dve, S["f_root"], t + 1)
                v.reciprocal(stat[:, 43:44], stat[:, 42:43])
                settle()
                v.scalar_tensor_tensor(h_row[:], xall[:, ds(t, 1), :].rearrange("p a d -> p (a d)"), stat[:, 43:44], g_ffn[:],
                                       ALU.mult, ALU.mult).then_inc(S["h_row"], 1)
                yield

            def choose_experts(t, others):
                hold(dve, S["s_kept"], 4 * t + 4)
                dve.sem_inc(S["dve_past"], 1)

                def top16(values, indices, scores, n, others=iter(())):
                    for x in range(n):
                        v.max(values(x)[:, 0:8], scores(x))
                    settle()
                    for x in range(n):
                        v.max_index(indices(x)[:, 0:8], values(x)[:, 0:8], scores(x))
                    settle()
                    for x in range(n):
                        v.match_replace(scores(x), values(x)[:, 0:8], scores(x), TAKEN)
                    settle()
                    next(others, None)
                    for x in range(n):
                        v.max(values(x)[:, 8:16], scores(x))
                    settle()
                    next(others, None)
                    for x in range(n):
                        v.max_index(indices(x)[:, 8:16], values(x)[:, 8:16], scores(x))
                    settle()
                    next(others, None)

                at = [(4 * (x // 8) + x % 4, x // 4 % 2) for x in range(2 * PH)]
                top16(lambda x: sv[:, at[x][0], at[x][1], :], lambda x: si[:, at[x][0], at[x][1], :], lambda x: s_pk[:, x, :], 2 * PH, others)
                dve.sem_inc(S["s_free"], 1)
                v.tensor_tensor(cand[:].rearrange("p h (i j) -> p h i j", i=TK), sv[:, :, 0, :].unsqueeze(3).broadcast_to([P, PH, TK, TK]),
                                sv[:, :, 1, :].unsqueeze(2).broadcast_to([P, PH, TK, TK]), ALU.add)
                v.tensor_copy(sif[:], si[:])
                settle()
                top16(lambda x: cv[:, x, :], lambda x: ci[:, x, :], lambda x: cand[:, x, :], PH)
                v.tensor_scalar(ci2[:], ci[:], TK - 1, None, ALU.bitwise_and)
                v.tensor_scalar(ci[:], ci[:], 4, None, ALU.logical_shift_right)
                settle()
                v.tensor_copy(cif[:, 0], ci[:])
                v.tensor_copy(cif[:, 1], ci2[:])
                settle()
                for half in range(2):
                    place = cif[:, half].rearrange("p h k -> p (h k)").unsqueeze(2).broadcast_to([P, PH * TK, TK])
                    v.tensor_tensor(hot[:], place, iota16[:].unsqueeze(1).broadcast_to([P, PH * TK, TK]), ALU.is_equal)
                    settle()
                    hot4 = hot[:].rearrange("p (h k) j -> p h k j", h=PH)
                    v.tensor_tensor(hot4, hot4, sif[:, :, half, :].unsqueeze(2).broadcast_to([P, PH, TK, TK]), ALU.mult)
                    settle()
                    v.tensor_reduce(esel[:, half], hot4, AX, ALU.add)
                    settle()
                v.scalar_tensor_tensor(experts[:, ds(t, 1), :], esel[:, 0:1].rearrange("p a h k -> p a (h k)"), float(NK),
                                       esel[:, 1:2].rearrange("p a h k -> p a (h k)"), ALU.mult, ALU.add)
                v.tensor_copy(m_gate[:], cv[:, :, 0:1].rearrange("p h a -> p (h a)"))
                settle()
                v.tensor_tensor(cv[:], cv[:], m_gate[:].unsqueeze(2).broadcast_to([P, PH, TK]), ALU.subtract).then_inc(S["f_centered"], 1)
                hold(dve, S["f_exped"], t + 1)
                v.tensor_reduce(m_gate[:], cv[:], AX, ALU.add)
                settle()
                v.reciprocal(m_gate[:], m_gate[:])
                settle()
                v.tensor_tensor(gates[:, ds(t, 1), :].rearrange("p a (h k) -> p (a h) k", h=PH), cv[:], m_gate[:].unsqueeze(2).broadcast_to([P, PH, TK]), ALU.mult)
                settle()

            def all_of(steps):
                for _ in steps:
                    pass

            all_of(mix(0))
            with dve.Fori(0, NTILE - 2) as t:
                choose_experts(t, mix(t + 1))
            choose_experts(NTILE - 2, iter(()))
            meet(dve, 4)
            pool_ready(dve, 3)

            def softmax(n, width, went, f):
                v.tensor_reduce(m_s[:], s_s[:].rearrange("p g c -> p c g"), AX, ALU.max).then_inc(S["m_part"], 1)
                went(f + 0.030)
                hold(dve, S["m_turned"], n)
                v.tensor_reduce(stat[0:NTOK, 20:21], ps[5][0:NTOK, 0:P], AX, ALU.max)
                settle()
                v.tensor_scalar(m_diag[0:NTOK, :], ident[0:NTOK, 0:NTOK], stat[0:NTOK, 20:21], None, ALU.mult).then_inc(S["m_diag"], 1)
                went(f + 0.060)
                hold(dve, S["m_all"], n)
                v.tensor_tensor(s_s[:], s_s[:], ps[5][:, P:P + NTOK].unsqueeze(1).broadcast_to([P, NPG + 1, NTOK]), ALU.subtract).then_inc(S["centered"], 1)
                went(f + 0.090)
                hold(dve, S["weighted"], n)
                v.reciprocal(stat[0:NTOK, 21:22], ps[4][0:NTOK, width:width + 1])
                settle()
                v.tensor_scalar(o_s[0:NTOK, 0:width], ps[4][0:NTOK, 0:width], stat[0:NTOK, 21:22], None, ALU.mult).then_inc(S["o_scaled"], 1)
                settle()

            def sample_attention(b, went):
                went(0.12)
                hold(dve, S["a_scored"], b + 1)
                for q, (g0, n) in enumerate(group_cols(NPG + 1, 8)):
                    m = sel_s[:, g0:g0 + n, ds(b * NT, NT)].unsqueeze(2).broadcast_to([P, n, HA, NT])
                    v.tensor_tensor(s_s[:, g0:g0 + n, :].rearrange("p g (h t) -> p g h t", h=HA),
                                    s_bank(q)[:, 0:n * NTOK].rearrange("p (g h t) -> p g h t", g=n, h=HA), m, ALU.add)
                settle()
                softmax(SOFT * b + 1, P, went, 0.12)
                hold(dve, S["pe_in"], 16 * (NPG + 1) * (b + 1))
                v.tensor_tensor(pe_sq[:], pe_s[:], pe_s[:], ALU.mult)
                settle()
                v.tensor_reduce(pe_norm[:], pe_sq[:], AX, ALU.add)
                for g in range(NPG + 1):
                    went(0.22 + 0.63 * (g + 0.7) / NPG)
                    hold(dve, S["squared"], (NPG + 1) * b + g + 1)
                    v.tensor_reduce(norm_s[:, g, :], sq_s[:, g % 2, :].rearrange("p (h d) -> p h d", h=HB), AX, ALU.add).then_inc(S["reduced"], 1)
                settle()
                v.tensor_tensor(norm_s[:], norm_s[:], pe_norm[:].unsqueeze(2).broadcast_to([P, NPG + 1, HB]), ALU.add)
                settle()
                v.tensor_scalar(norm_s[:], norm_s[:], 1.0 / DQK, EPS, ALU.mult, ALU.add).then_inc(S["b_mean"], 1)
                went(0.88)
                hold(dve, S["b_root"], b + 1)
                v.reciprocal(norm_s[:], norm_s[:])
                settle()
                hold(dve, S["b_scored"], b + 1)
                for q, (g0, n) in enumerate(group_cols(NPG + 1, 8)):
                    v.tensor_tensor(s_s[:, g0:g0 + n, :].rearrange("p g (h t) -> p g h t", h=HB),
                                    s_bank(q)[:, 0:n * NTOK].rearrange("p (g h t) -> p g h t", g=n, h=HB),
                                    norm_s[:, g0:g0 + n, :].unsqueeze(3).broadcast_to([P, n, HB, NT]), ALU.mult)
                settle()
                last = s_s[:, NPG, :].rearrange("p (h t) -> p h t", h=HB)
                v.tensor_tensor(last, last, new_keys[:].unsqueeze(1).broadcast_to([P, HB, NT]), ALU.add)
                settle()
                softmax(SOFT * b + 2, DC, went, 0.88)

            def dots(t, n0, n1):
                for n in range(n0, n1):
                    r = n % NRING
                    hold(dve, landed[r], 16 * (32 * t + n // NRING + 1))
                    v.scalar_tensor_tensor(ring[:, r, :], ring[:, r, :], 1.0, h_cur[:], ALU.mult, ALU.mult,
                                           accum_out=acts[:, n:n + 1]).then_inc(freed[r], 1)

            def sums(t, cols, m0, m1):
                for m in range(m0, m1):
                    if m % EACH == 0:
                        continue
                    r = m % NRING
                    hold(dve, landed[r], 16 * (32 * t + (cols + m) // NRING + 1))
                    if m == 1:
                        v.tensor_scalar(acc[:], ring[:, r, :], wts[:, m:m + 1], None, ALU.mult).then_inc(freed[r], 1)
                    else:
                        v.scalar_tensor_tensor(acc[:], ring[:, r, :], wts[:, m:m + 1], acc[:], ALU.mult, ALU.add).then_inc(freed[r], 1)
                    settle()

            def in_parts(work, cols):
                done = [0]

                def went(f):
                    upto = min(cols, int(cols * f) // 2 * 2)
                    if upto > done[0]:
                        work(done[0], upto)
                        done[0] = upto
                return went

            def weights(t, cols):
                settle()
                dve.sem_inc(S["dotted"], 1)
                hold(dve, S["gelu"], t + 1)

            for r in range(NRING):
                dve.sem_inc(freed[r], 1)
            dve.sem_inc(S["y_read"], 1)
            v.tensor_copy(e_u[:], experts[:, 0, :]).then_inc(S["e_u"], 1)
            with dve.Fori(0, NTILE - 1) as t:
                v.tensor_copy(h_cur[:].rearrange("p (c k) -> p c k", c=KD), oT[:, :, ds(t * P, P)])
                v.tensor_copy(e_v[:], experts[:, ds(t, 1), :].rearrange("p a k -> p (a k)")).then_inc(S["e_v"], 1)
                settle()
                went = in_parts(lambda n0, n1: dots(t, n0, n1), P)
                sample_attention(2 * t, went)
                went(1)
                weights(t, P)
                v.tensor_tensor(wts[:], acts[:], gates[:, ds(t, 1), :].rearrange("p a k -> p (a k)"), ALU.mult).then_inc(S["wts"], 1)
                v.tensor_copy(e_u[:], experts[:, ds(t + 1, 1), :].rearrange("p a k -> p (a k)")).then_inc(S["e_u"], 1)
                settle()
                went = in_parts(lambda m0, m1: sums(t, P, m0, m1), P)
                sample_attention(2 * t + 1, went)
                went(1)
                hold(dve, S["y_out"], 16 * (t + 1))
                v.tensor_tensor(y_cur[:], acc[:], xall[:, ds(t, 1), :].rearrange("p a d -> p (a d)"), ALU.add)
                settle()
                hold(dve, S["v_done"], t + 1)
                for j in range(2):
                    last = v.tensor_tensor(y_cur[:, 512 * j:512 * j + 512], y_cur[:, 512 * j:512 * j + 512], ps[6 + j][:], ALU.add)
                last.then_inc(S["y_ready"], 1)
                settle()
                dve.sem_inc(S["y_read"], 1)
            meet(dve, 5)
            dve.wait_ge(S["f_weights"], NFW + 16 * 4)
            all_of(mix(NTILE - 1))
            choose_experts(NTILE - 1, iter(()))
            meet(dve, 6)
            t, cols = NTILE - 1, P // 2
            v.tensor_copy(h_cur[:].rearrange("p (c k) -> p c k", c=KD), oT[:, :, t * P:(t + 1) * P])
            for ids, name in ((e_u, "e_u"), (e_v, "e_v")):
                for half in range(2):
                    rows = slice(NTOK * half, NTOK * half + NTOK)
                    last = v.tensor_copy(ids[rows, 0:cols], experts[rows, t, cols * half:cols * half + cols])
                last.then_inc(S[name], 1)
            settle()
            dots(t, 0, cols)
            weights(t, cols)
            for half in range(2):
                rows = slice(NTOK * half, NTOK * half + NTOK)
                last = v.tensor_tensor(wts[rows, 0:cols], acts[rows, 0:cols], gates[rows, t, cols * half:cols * half + cols], ALU.mult)
            last.then_inc(S["wts"], 1)
            settle()
            sums(t, cols, 0, cols)
            dve.sem_inc(S["acc_done"], 1)
            dve.wait_ge(S["v_done"], NTILE)
            for j in range(2):
                last = v.tensor_tensor(y_cur[0:NTOK, 512 * j:512 * j + 512], xall[0:NTOK, t, 512 * j:512 * j + 512], ps[6 + j][0:NTOK, :], ALU.add)
            last.then_inc(S["y_ready"], 1)

        @block.tensor
        def _(pe):
            te = nc.tensor
            pe.wait_ge(weights_in, 64)
            pe.wait_ge(const_in, NCONST)
            with pe.Fori(0, NTILE) as t:
                hold(pe, x_normed, t + 1)
                for c in range(KD):
                    last = te.transpose(ps[c // 4][:, (c % 4) * P:(c % 4 + 1) * P], xn[:, c * P:(c + 1) * P], ident[:])
                last.then_inc(x_turned, 1)
                hold(pe, xT_ready, t + 1)
                for i, (c0, w) in enumerate(group_cols(DIN)):
                    for c in range(KD):
                        last = te.matmul(ps[2 + i][:, 0:w], xT[:, c, :], w_in[:, c, c0:c0 + w], start=(c == 0), stop=(c == KD - 1))
                    last.then_inc(proj_done, 1)
                hold(pe, cur_normed, t + 1)
                for g in range(G):
                    te.transpose(ps[0][:, g * P:(g + 1) * P], cur[:, g * P:(g + 1) * P], ident[:])
                te.transpose(ps[1][:, 0:P], cur[:, OKA:OKA + P], ident[:])
                for c in range(3):
                    te.transpose(ps[1][:, (c + 1) * P:(c + 2) * P], cur[:, OCQ + c * P:OCQ + (c + 1) * P], ident[:])
                for c in range(2):
                    te.transpose(ps[6][:, c * P:(c + 1) * P], cur[:, OCKV + c * P:OCKV + (c + 1) * P], ident[:])
                te.transpose(ps[6][:, 2 * P:3 * P], ki2[:], ident[:])
                for c in range(2):
                    last = te.transpose(ps[7][:, c * P:(c + 1) * P], cur[:, OQI + c * P:OQI + (c + 1) * P], ident[:])
                last.then_inc(cur_turned, 1)
                hold(pe, latents_ready, t + 1)
                for c in range(3):
                    te.matmul(ps[2][:], cqT[:, c, :], w_uq[:, c, 0:512], start=(c == 0), stop=(c == 2))
                for c in range(3):
                    te.matmul(ps[3][:, 0:256], cqT[:, c, :], w_uq[:, c, 512:768], start=(c == 0), stop=(c == 2))
                for c in range(2):
                    te.matmul(ps[4][:], ckvT[:, c, :], w_uk[:, c, :], start=(c == 0), stop=(c == 1))
                for c in range(2):
                    last = te.matmul(ps[5][:], ckvT[:, c, :], w_uv[:, c, :], start=(c == 0), stop=(c == 1))
                last.then_inc(up_done, 1)
                hold(pe, up_normed, t + 1)
                for h in range(HB):
                    te.transpose(ps[h // 4][0:DQK, (h % 4) * P:(h % 4 + 1) * P], qb[:, h, :], ident[:])
                for h in range(HB):
                    last = te.transpose(ps[2 + h // 4][0:DQK, (h % 4) * P:(h % 4 + 1) * P], kb[:, h, :], ident[:])
                last.then_inc(up_turned, 1)
            meet(pe, 1)
            pe.wait_ge(S["w_diag"], 1)
            te.matmul(ps[6][:, 0:HI * NTOK], ones[0:NTOK, :], w_diag[0:NTOK].rearrange("p h t -> p (h t)"), start=True, stop=True).then_inc(S["w_bcast"], 1)
            for i in range(2):
                for h in range(4):
                    for c in range(2):
                        last = te.transpose(ps[h // 2][0:DN, (h % 2) * DC + c * P:(h % 2) * DC + (c + 1) * P], w_uk[:, c, (4 * i + h) * DN:(4 * i + h + 1) * DN], ident[:])
                last.then_inc(S["uk_turned"], 1)
                pe.wait_ge(S["uk_ready"], i + 1)
                for h in range(4):
                    for c in range(2):
                        last = te.matmul(ps[2 + i][:, (2 * h + c) * NTOK:(2 * h + c + 1) * NTOK], ukT[0:DN, h, c * P:(c + 1) * P],
                                         qbT[0:DN, 4 * i + h, SAMP:SAMP + NTOK], start=True, stop=True)
                last.then_inc(S["q_lat"], 1)
            pe.wait_ge(S["qabs_ready"], 2)
            pe.wait_ge(S["qi_ready"], 1)
            pe.sem_inc(S["kidx_free"], 2)
            with pe.Fori(0, NB // 2) as bb:
                for e in range(2):
                    b = 2 * bb + e
                    for queue in ("sp", "pool"):
                        hold(pe, S[f"kidx_{queue}{e}"], 16 * NPG // 2 * (bb + 1))
                        pe.sem_inc(S["pe_past"], 1)
                    for g in range(NPG):
                        last = te.transpose(ps[g // 4][0:DI, (g % 4) * P:(g % 4 + 1) * P], kidx[e][:, g, :], ident[:])
                    last.then_inc(S["i_turned"], 1)
                    hold(pe, S["i_ready"], b + 1)
                    pe.sem_inc(S["kidx_free"], 1)
                    hold(pe, S["i_free"], b + 1)
                    q = qi_s[0:DI, :, ds(b * NT, NT)]
                    for g in range(NPG + 1):
                        dst = (ps[4][:, g * 32:g * 32 + 32] if g < NPG else ps[5][:, 0:32]).rearrange("p (h t) -> p h t", h=HI)
                        last = te.matmul(dst, kidxT[0:DI, g, :], q, start=True, stop=True)
                    last.then_inc(S["i_scored"], 1)
            pe.wait_ge(S["i_summed"], 1)
            for g in range(NPG + 1):
                dst = ps[g // 4][0:NTOK, (g % 4) * P:(g % 4 + 1) * P] if g < NPG else ps[5][0:NTOK, 0:P]
                last = te.transpose(dst, i_all[:, g, :], ident[:])
            last.then_inc(S["i_rows"], 1)
            meet(pe, 2)
            with pe.Fori(0, 4) as i:
                hold(pe, S["idx_q"], i + 1)
                for h in range(HI):
                    b = slice(64 * (h % 2), 64 * (h % 2) + 64)
                    te.matmul(ps[h][:], q_idx[b, h // 2, :], kiT[b, 0:SEQ], start=True, stop=True).then_inc(S["idx_scored"], 1)

            def attention(first, scores, values):
                with pe.Fori(0, 4) as g:
                    n0 = first + 8 * g

                    def score(u):
                        if u >= 2:
                            hold(pe, S["exped"], n0 + u - 1)
                        scores(g, u, *UNITS[u]).then_inc(S["scored"], 1)

                    hold(pe, S["head_q"], g + 1 + first // 8)
                    score(0)
                    for u, (blk, c) in enumerate(UNITS):
                        if u < 7:
                            score(u + 1)
                        else:
                            pe.sem_inc(S["head_done"], 1)
                        hold(pe, S["exped"], n0 + u + 1)
                        for k in range(blk + 1):
                            last = te.transpose(ps[2 + u % 2][:, k * P:(k + 1) * P], p_cur[:, u % 2, k * P:(k + 1) * P], ident[:])
                        last.then_inc(S["p_turned"], 1)
                        hold(pe, S["pT_ready"], n0 + u + 1)
                        for k in range(blk + 1):
                            last = te.matmul(ps[4 + u % 2][:, 0:64], pT[:, u % 2, k * P:(k + 1) * P], values(g, c, k), start=(k == 0), stop=(k == blk))
                        last.then_inc(S["attended"], 1)
                    hold(pe, S["normed_o"], n0 + 8)
                    for blk in range(4):
                        last = te.transpose(ps[6][:, blk * P:(blk + 1) * P], o_pair[:, blk, :], ident[:])
                    last.then_inc(S["pair_turned"], 1)

            def scores_a(g, u, blk, c):
                b = slice(64 * c, 64 * c + 64)
                return te.matmul(ps[u % 2][:, 0:(blk + 1) * P], q_cur[b, 0, blk * P:(blk + 1) * P], kaT[b, 0:(blk + 1) * P], start=True, stop=True)

            def scores_b(g, u, blk, c):
                keys = kbT[:, ds(2 * g + c, 1), 0:(blk + 1) * P].rearrange("p a b -> p (a b)")
                return te.matmul(ps[u % 2][:, 0:(blk + 1) * P], q_cur[0:DQK, c, blk * P:(blk + 1) * P], keys, start=True, stop=True)

            attention(0, scores_a, lambda g, c, k: va[:, k, c * DH:(c + 1) * DH])
            attention(32, scores_b, lambda g, c, k: vb[:, k, ds((2 * g + c) * DV, DV)])
            pe.wait_ge(S["i_chosen"], 1)
            for g in range(NPG + 1):
                last = te.transpose(ps[g // 8][:, (g % 8) * NTOK:(g % 8 + 1) * NTOK], i_row[0:NTOK, g * P:(g + 1) * P], ident[0:NTOK, 0:NTOK])
            last.then_inc(S["i_back"], 1)
            meet(pe, 3)
            pe.wait_ge(S["f_weights"], NFW)
            for h in range(PH):
                last = te.transpose(ps[h // 4][:, (h % 4) * P:(h % 4 + 1) * P], sk[:, 2 * h:2 * h + 2, :].rearrange("p a d -> p (a d)"), ident[:])
            last.then_inc(S["sk_turned"], 1)
            pe.wait_ge(S["skT_ready"], 1)

            def route(t):
                hold(pe, S["o_cur"], t + 1)
                for j in range(2):
                    for c in range(KD):
                        last = te.matmul(ps[j][:], o_cur[:, c, :], w_out[:, c, 512 * j:512 * j + 512], start=(c == 0), stop=(c == KD - 1))
                    last.then_inc(S["o_up"], 1)
                hold(pe, S["h_row"], t + 1)
                for c in range(KD):
                    last = te.transpose(ps[2 + c // 4][:, (c % 4) * P:(c % 4 + 1) * P], h_row[:, c * P:(c + 1) * P], ident[:])
                last.then_inc(S["h_turned"], 1)
                hold(pe, S["h2T"], t + 1)
                for h in range(PH):
                    for c in range(KD):
                        last = te.matmul(ps[4 + h // 4][:, (h % 4) * P:(h % 4 + 1) * P], w_pq[:, c, h * P:(h + 1) * P], h2T[:, c, :], start=(c == 0), stop=(c == KD - 1))
                    if h % 4 == 3:
                        last.then_inc(S["q_up"], 1)
                for j, bank in enumerate((0, 1, 6, 7)):
                    if j % 2 == 0:
                        hold(pe, S["q_kept"], 2 * t + j // 2 + 1)
                    for x in range(4):
                        h, half = 4 * (j // 2) + x, j % 2
                        r = slice(64 * half, 64 * half + 64)
                        last = te.matmul(ps[bank][:, x * P:(x + 1) * P], qpT[r, h, :], skT[r, h, :], start=True, stop=True)
                    last.then_inc(S["routed"], 1)

            with pe.Fori(0, NTILE - 1) as t:
                route(t)
            meet(pe, 4)
            pool_ready(pe, 3)

            def softmax(n, values, width, chunks, free, went, f):
                went(f + 0.025)
                hold(pe, S["m_part"], n)
                pe.sem_inc(S["pe_past"], 1)
                te.transpose(ps[5][0:NTOK, 0:P], m_s[:], ident[:]).then_inc(S["m_turned"], 1)
                went(f + 0.050)
                hold(pe, S["m_diag"], n)
                te.matmul(ps[5][:, P:P + NTOK], ones[0:NTOK, :], m_diag[0:NTOK, :], start=True, stop=True).then_inc(S["m_all"], 1)
                went(f + 0.075)
                hold(pe, S["s_exped"], n)
                for g in range(NPG + 1):
                    last = te.matmul(ps[4][0:NTOK, 0:width + 1], s_s[:, g, :], values[:, g, :], start=(g == 0), stop=(g == NPG))
                last.then_inc(S["weighted"], 1)
                went(f + 0.100)
                hold(pe, S["o_scaled"], n)
                pe.sem_inc(S[free], 1)
                for c in range(chunks):
                    last = te.transpose(ps[5][:, c * NTOK:(c + 1) * NTOK], o_s[0:NTOK, c * P:(c + 1) * P], ident[0:NTOK, 0:NTOK])
                last.then_inc(S["o_turned"], 1)
                hold(pe, S["o_kept"], n)

            def sample_attention(b, went):
                def s_dst(g):
                    return s_bank(g // 8)[:, g % 8 * NTOK:(g % 8 + 1) * NTOK]

                hold(pe, S["k_in"], 16 * (NPG + 1) * (b + 1))
                hold(pe, S["q_blk"], b + 1)
                for q, (g0, n) in enumerate(group_cols(NPG + 1, 4)):
                    for g in range(n):
                        last = te.transpose(ps[q % 2][:, g * P:(g + 1) * P], k_s[:, g0 + g, :], ident[:])
                    last.then_inc(S["k_turned"], 1)
                    went(0.12 * (q + 1) / 5)
                    hold(pe, S["k_ready"], 5 * b + q + 1)
                    for g in range(g0, g0 + n):
                        last = te.matmul(s_dst(g), kT_s[:, q % 2, g - g0, :], q_blk[:], start=True, stop=True)
                last.then_inc(S["a_scored"], 1)
                pe.sem_inc(S["k_free"], 1)
                hold(pe, S["v_in"], 16 * (NPG + 1) * (b + 1))
                softmax(SOFT * b + 1, v_s, P, 1, "v_free", went, 0.12)
                pe.sem_inc(S["q_free"], 1)
                hold(pe, S["c_in"], 16 * (NPG + 1) * (b + 1))
                hold(pe, S["pe_in"], 16 * (NPG + 1) * (b + 1))

                def turn(g):
                    bank = ps[g % 2]
                    te.transpose(bank[:, 0:P], c_s[:, g, 0:P], ident[:])
                    te.transpose(bank[:, P:2 * P], c_s[:, g, P:2 * P], ident[:])
                    te.transpose(bank[0:DR, 2 * P:3 * P], pe_s[:, g, :], ident[:]).then_inc(S["c_turned"], 1)

                turn(0)
                for g in range(NPG + 1):
                    n = (NPG + 1) * b + g + 1
                    if g < NPG:
                        if g >= 1:
                            hold(pe, S["c_ready"], n - 1)
                        turn(g + 1)
                    went(0.22 + 0.63 * g / NPG)
                    hold(pe, S["c_ready"], n)
                    dst = s_dst(g)
                    cols = ds(b * NT, NT)
                    dst = dst.rearrange("p (h t) -> p h t", h=HB)
                    te.matmul(dst, cT_s[:, g % 2, 0, :], qabs[:, 0, :, cols], start=True, stop=False)
                    te.matmul(dst, cT_s[:, g % 2, 1, :], qabs[:, 1, :, cols], start=False, stop=False)
                    te.matmul(dst, cT_s[0:DR, g % 2, 2, :], q_pe[0:DR, :, ds(b * NT, NT)], start=False, stop=True)
                    if g >= 1:
                        hold(pe, S["squared"], n - 1)
                    bank = ps[4]
                    for c in range(2):
                        last = te.matmul(bank[:], cT_s[:, g % 2, c, :], w_uk[:, c, :], start=(c == 0), stop=(c == 1))
                    last.then_inc(S["nope"], 1)
                pe.sem_inc(S["b_scored"], 1)
                pe.sem_inc(S["pe_free"], 1)
                softmax(SOFT * b + 2, c_s, DC, 2, "c_free", went, 0.88)

            def sums(t, cols, width, m0, m1):
                for m in range(-(-m0 // EACH) * EACH, m1, EACH):
                    r = m % NRING
                    if m == 0:
                        hold(pe, S["y_read"], t + 1)
                    hold(pe, S["diag"], P // EACH * t + m // EACH + 1)
                    hold(pe, landed[r], 16 * (32 * t + (cols + m) // NRING + 1))
                    for j in range(2):
                        last = te.matmul(ps[6 + j][0:width, :], diag[:, m // EACH % NDIAG, 0:width], ring[:, r, 512 * j:512 * j + 512],
                                         start=(m == 0), stop=(m == cols - EACH and width == P), skip_group_check=True)
                    last.then_inc(freed[r], 1)

            def in_parts(work, cols):
                done = [0]

                def went(f):
                    upto = min(cols, int(cols * f) // 2 * 2)
                    if upto > done[0]:
                        work(done[0], upto)
                        done[0] = upto
                return went

            for name in ("k_free", "v_free", "c_free", "pe_free", "q_free"):
                pe.sem_inc(S[name], 1)
            with pe.Fori(0, NTILE - 1) as t:
                sample_attention(2 * t, lambda f: None)
                went = in_parts(lambda m0, m1: sums(t, P, P, m0, m1), P)
                sample_attention(2 * t + 1, went)
                went(1)
                pe.drain()
                pe.sem_inc(S["v_done"], 1)
            for j in range(4):
                for c in range(2):
                    last = te.matmul(ps[0][:, j * P:(j + 1) * P], w_uv[:, c, j * P:(j + 1) * P], olT[:, c, 2 * j:2 * j + 2, :].rearrange("p h t -> p (h t)"), start=(c == 0), stop=(c == 1))
            last.then_inc(S["v_lat"], 1)
            meet(pe, 5)
            pe.wait_ge(S["f_weights"], NFW + 16 * 4)
            route(NTILE - 1)
            meet(pe, 6)
            t, cols = NTILE - 1, P // 2
            sums(t, cols, NTOK, 0, cols)
            pe.wait_ge(S["acc_done"], 1)
            for j in range(2):
                last = te.matmul(ps[6 + j][0:NTOK, :], fold[:], acc[:, 512 * j:512 * j + 512], start=False, stop=True, skip_group_check=True)
            last.then_inc(S["v_done"], 1)


_INS = ["x_prompt", "x_sample", "cache_a_k", "cache_a_v", "cache_a_kidx", "cache_b_ckv", "cache_b_kpe", "page_table",
        "g_norm_mix", "w_in", "g_q_a", "g_k_a", "g_k_idx", "g_cq", "w_uq", "g_ckv", "w_uk", "w_uv", "g_q_b", "g_k_b",
        "w_out", "g_norm_ffn", "w_peer_q", "peer_sub_keys", "peer_u", "peer_v"]
_OUTS = [("p_y", (SEQ, D)), ("s_y", (NTOK, D)),
         ("p_a_k", (SEQ, 128)), ("p_a_v", (SEQ, 128)), ("p_a_kidx", (SEQ, DI)), ("p_b_ckv", (SEQ, DC)), ("p_b_kpe", (SEQ, DR)),
         ("s_a_k", (NTOK, 128)), ("s_a_v", (NTOK, 128)), ("s_a_kidx", (NTOK, DI)), ("s_b_ckv", (NTOK, DC)), ("s_b_kpe", (NTOK, DR))]
_SHAPES = [(1, SEQ, D), (NB, NT, D), (1, SEQ, KVA, DH), (1, SEQ, KVA, DH), (1, SEQ, DI), (1, SEQ, DC), (1, SEQ, DR),
           (NB, NT, KVA, DH), (NB, NT, KVA, DH), (NB, NT, DI), (NB, NT, DC), (NB, NT, DR)]


def shape_constants():
    import numpy as np

    f = np.float32
    pos = np.zeros((NTILE, P), f)
    pos[:NTILE - 1] = np.arange(SEQ, dtype=f).reshape(NTILE - 1, P)
    pos[NTILE - 1, :NTOK] = np.tile(PAST + np.arange(NT, dtype=f), NB)

    def rope(n_rot):
        half = n_rot // 2
        inv = (f(THETA) ** (-np.arange(half, dtype=f) * f(2.0) / f(n_rot))).astype(f)
        ang = (pos[:, :, None] * inv[None, None, :]).astype(f)
        tab = np.stack([np.cos(ang), np.sin(ang)]).astype(f)
        return np.ascontiguousarray(tab.transpose(2, 0, 1, 3))

    j = np.arange(SEQ + 384)[None, :] - 384
    causal = np.where(j <= np.arange(P)[:, None], 0.0, NEG).astype(f)
    key = np.arange(P)[:, None]
    new_keys = np.where(key <= np.arange(NT)[None, :], 0.0, NEG).astype(f)
    new_rows = np.where(np.arange(NT)[None, :] <= np.arange(NTOK)[:, None] % NT, 0.0, NEG).astype(f)
    return {"c_fold": np.tile(np.eye(NTOK, dtype=f), (2, 1)), "c_ones": np.ones((P, P), f), "c_new_keys": new_keys, "c_new_rows": new_rows, "c_iota16": np.tile(np.arange(TK, dtype=f), (P, 1)),
            "c_ident": np.eye(P, dtype=f), "c_rope_a": rope(16), "c_rope_b": rope(32), "c_causal": causal}


def kernel(**inputs):
    import numpy as _np
    import concourse.bacc as _bacc
    from concourse import mybir as _mybir
    from concourse.bass_utils import run_bass_kernel_spmd as _run

    nc = _bacc.Bacc("TRN2", target_bir_lowering=False, num_devices=1)
    arrays, aps = {}, {}
    for name in _INS:
        arrays[name] = _np.ascontiguousarray(inputs[name])
    arrays.update(shape_constants())
    for name, x in arrays.items():
        aps[name] = nc.dram_tensor("in_" + name, x.shape, _mybir.dt.from_np(x.dtype), kind="ExternalInput").ap()
    outs = {n: nc.dram_tensor("out_" + n, s, _mybir.dt.float32, kind="ExternalOutput").ap() for n, s in _OUTS}
    program(nc, aps, outs)
    r = _run(nc, [{"in_" + n: x for n, x in arrays.items()}], core_ids=[0]).results[0]
    return tuple(r["out_" + n].reshape(s) for (n, _), s in zip(_OUTS, _SHAPES))
```

```python
from contextlib import ExitStack

import concourse.bass as bass
from concourse import mybir

F32 = mybir.dt.float32
I32 = mybir.dt.int32
U32 = mybir.dt.uint32
ALU = mybir.AluOpType
ACT = mybir.ActivationFunctionType
AX = mybir.AxisListType.X
ds = bass.ds

P = 128
D = 1024
SEQ = 512
NB, NT = 8, 8
NTOK = NB * NT
PAST = 2048
PAGE = 128
NPG = PAST // PAGE
NPHYS = 160
HA, KVA, DH = 8, 2, 64
HI, DI = 4, 64
HB, DN, DR, DV = 8, 64, 32, 64
DQK = DN + DR
DCQ, DC = 384, 256
PH, NK, DK, TK = 8, 128, 128, 16
WIDTHS = (HA * DH, KVA * DH, KVA * DH, HI * DI, DI, HI, DCQ, DC, DR)
DIN = sum(WIDTHS)
OQA, OKA, OVA, OQI, OKI, OWI, OCQ, OCKV, OKPE = (sum(WIDTHS[:i]) for i in range(9))
KD = D // P
NTILE = SEQ // P + 1
NCOL = NTILE * P
SAMP = SEQ
EPS = 1e-6
NEG = -1e30
TAKEN = -3e38
G = HA // KVA
KTOP_P = min(256, SEQ // 4)
KTOP_S = min(256, (PAST + NT) // 4)
THETA = 500000.0


def group_cols(n, width=512):
    return [(c, min(width, n - c)) for c in range(0, n, width)]


def program(nc, a, o):
    ctx = ExitStack()
    with ctx:
        def sb(name, shape, dt=F32):
            return ctx.enter_context(nc.sbuf_tensor(name, shape, dt))

        def sem(name):
            return ctx.enter_context(nc.semaphore(name))

        ident = sb("ident", [P, P])
        ones = sb("ones", [P, P])
        rope_a = sb("rope_a", [P, 2, NTILE, 8])
        rope_b = sb("rope_b", [P, 2, NTILE, 16])
        causal = sb("causal", [P, SEQ + 384])
        g_mix_col = sb("g_mix_col", [P, KD])
        g_cq_col = sb("g_cq_col", [P, DCQ // P])
        fold = sb("fold", [P, NTOK])
        new_keys = sb("new_keys", [P, NT])
        new_rows = sb("new_rows", [NTOK, NT])
        pages = sb("pages", [1, NB * NPG], I32)
        stat = sb("stat", [P, 64])
        xall = sb("xall", [P, NTILE, D])
        w_uk = sb("w_uk_s", [P, DC // P, HB * DN])
        w_uv = sb("w_uv_s", [P, DC // P, HB * DV])

        class Region:

            def __init__(self, name, size):
                self.t, self.size, self.at = sb(name, [P, size]), size, 0

            def restart(self, at=0):
                self.at = at

            def view(self, *shape, parts=P, dt=F32):
                n = 1
                for w in shape:
                    n *= w
                x = self.t[0:parts, self.at:self.at + n]
                self.at += n
                assert self.at <= self.size, (self.at, self.size)
                if dt != F32:
                    x = x.bitcast(dt)
                names = "abcd"[:len(shape)]
                if len(shape) > 1:
                    x = x.rearrange(f"p ({' '.join(names)}) -> p {' '.join(names)}", **dict(zip(names, shape)))
                return x

        kept = Region("kept", 18580)
        qaT = kept.view(G, NCOL)
        kaT = kept.view(NCOL)
        qiT = kept.view(2, NCOL)
        kiT = kept.view(NCOL)
        qbT = kept.view(HB, NCOL, parts=DQK)
        kbT = kept.view(HB, NCOL, parts=DQK)
        va = kept.view(NTILE, KVA * DH)
        vb = kept.view(NTILE, HB * DV)
        wi = kept.view(NTILE, HI)

        work = Region("work", 24260)
        w_in = work.view(KD, DIN)
        w_uq = work.view(DCQ // P, HB * DQK)
        cur = work.view(DIN)
        xn = work.view(D)
        xT = work.view(KD, P)
        cqT = work.view(DCQ // P, P)
        ckvT = work.view(DC // P, P)
        qk_at = work.at
        qb = work.view(HB, DQK)
        kb = work.view(HB, DQK)
        work.restart(qk_at)
        cur_sq = work.view(2 * HB * DQK)
        up_sq = cur[:, 0:2 * HB * DQK]
        ki2 = work.view(2 * DI)
        rt = work.view(4, 16 * 8)
        g_heads = work.view(HA + KVA, DH)
        g_kidx = work.view(DI)
        g_ckv = work.view(DC)
        g_qk = work.view(2, DQK)
        work.restart()
        oT = work.view(2 * G, NCOL)
        sel_s = work.view(NPG + 1, NTOK)
        w_all = work.view(NB, HI * NT)
        olT = work.view(2, HB, NTOK)
        qabs = work.view(2, HB, NTOK)
        qa_s = work.view(G, NTOK)
        q_pe = work.view(HB, NTOK)
        g_ffn = work.view(D)
        skT = work.view(PH, NK)
        iota16 = work.view(TK)
        AFTER_SEL = work.at
        i_row = work.view((NPG + 1) * P)
        assert KTOP_P == P
        sel = work.view(3, SEQ)
        AFTER_CHOICE = work.at
        w_diag = work.view(HI, NTOK)
        kidx = [work.view(NPG, DI) for _ in range(2)]
        kidxT = work.view(NPG + 1, P)
        relus_at = work.at
        relus = work.view(HI, SEQ)
        after_relus = work.at
        work.restart(relus_at)
        w_relu = work.view(NPG + 1, HI * NT)
        i_all = work.view(NPG + 1, NTOK)
        work.restart(after_relus)
        ukT = work.view(4, DC)
        qi_s = work.view(HI, NTOK)
        work.restart(AFTER_CHOICE)
        q_cur = work.view(2, SEQ)
        s_cur = work.view(2, SEQ)
        p_cur = work.view(2, SEQ)
        pT = work.view(2, SEQ)
        o_pair = work.view(4, P)
        work.restart(AFTER_SEL)
        k_s = work.view(NPG + 1, P)
        c_s = work.view(NPG + 1, DC + 1)
        pe_s = work.view(NPG + 1, DR)
        pe_sq = work.view(NPG + 1, DR)
        q_blk = work.view(NTOK)
        kT_s = work.view(2, 4, P)
        cT_s = work.view(2, 3, P)
        sq_s = work.view(2, HB * DN)
        s_s = work.view(NPG + 1, NTOK)
        norm_s = work.view(NPG + 1, HB)
        pe_norm = work.view(NPG + 1)
        m_s = work.view(NTOK)
        m_diag = work.view(NTOK)
        o_s = work.view(DC)
        kept.restart()
        w_out = kept.view(KD, D)
        assert G * D <= 2 * G * NCOL
        w_pq = kept.view(KD, D)
        experts = kept.view(NTILE, P, dt=U32)
        gates = kept.view(NTILE, P)
        work.restart(AFTER_SEL)
        o_cur = work.view(KD, P)
        h_row = work.view(D)
        h2T = work.view(KD, P)
        qpT = work.view(PH, P)
        sv = work.view(PH, 2, TK)
        si = work.view(PH, 2, TK, dt=U32)
        sif = work.view(PH, 2, TK)
        sk_at = work.at
        sk = work.view(PH * 2, DK // 2)
        work.restart(sk_at)
        cand = work.view(PH, TK * TK)
        s_pk = work.view(2 * PH, NK)
        cv = work.view(PH, TK)
        ci = work.view(PH, TK, dt=U32)
        ci2 = work.view(PH, TK, dt=U32)
        cif = work.view(2, PH, TK)
        hot = work.view(PH * TK, TK)
        esel = work.view(2, PH, TK)
        m_gate = work.view(PH)
        kept.restart()
        NRING = 8
        EACH = 4
        NDIAG = 4
        ring = kept.view(NRING, D)
        h_cur = kept.view(D)
        e_u = kept.view(P, dt=U32)
        e_v = kept.view(P, dt=U32)
        acts = kept.view(P)
        wts = kept.view(P)
        diag = kept.view(NDIAG, P)
        acc = kept.view(D)
        y_cur = kept.view(D)
        v_s = kept.view(NPG + 1, P + 1)
        assert kept.at <= 2 * KD * D

        ps = [ctx.enter_context(nc.psum_tensor(f"ps{i}", [P, 512], F32)) for i in range(8)]

        ident_in = sem("ident_in")
        g_mix_in = sem("g_mix_in")
        const_in = sem("const_in")
        w_in_in = [sem(f"w_in_in{i}") for i in range(len(group_cols(DIN)))]
        x_in = sem("x_in")
        weights_in = sem("weights_in")
        x_sum = sem("x_sum")
        x_mean = sem("x_mean")
        x_root = sem("x_root")
        x_normed = sem("x_normed")
        x_turned = sem("x_turned")
        xT_ready = sem("xT_ready")
        proj_done = sem("proj_done")
        cur_ready = sem("cur_ready")
        cur_mean = sem("cur_mean")
        cur_root = sem("cur_root")
        cur_normed = sem("cur_normed")
        cur_turned = sem("cur_turned")
        latents_ready = sem("latents_ready")
        up_done = sem("up_done")
        up_ready = sem("up_ready")
        up_mean = sem("up_mean")
        up_root = sem("up_root")
        up_normed = sem("up_normed")
        up_turned = sem("up_turned")
        tile_kept = sem("tile_kept")
        rows_out = sem("rows_out")

        rows_left = sem("rows_left")

        all_here = sem("all_here")
        S = {n: sem(n) for n in (
            "idx_scored", "idx_relu", "idx_summed", "head_q", "scored", "biased", "exped", "p_turned", "pT_ready",
            "attended", "normed_o", "inverted", "pair_turned", "pair_kept", "head_done", "pool_step", "pool_made", "q_free", "i_free", "pe_past",
            "kidx_sp0", "kidx_sp1", "kidx_pool0", "kidx_pool1", "kidx_free", "w_diag", "w_bcast", "w_ready", "uk_turned", "uk_ready", "q_lat", "qabs_ready", "qi_ready",
            "i_turned", "i_ready", "i_scored", "i_summed", "i_rows", "i_chosen", "i_back", "sel_ready",
            "k_in", "v_in", "c_in", "pe_in", "k_free", "v_free", "c_free", "pe_free", "q_blk", "k_turned", "k_ready", "a_scored",
            "c_turned", "c_ready", "nope", "squared", "b_scored", "b_mean", "b_root", "reduced",
            "sk_in", "w_out_a_in", "w_out_b_in", "g_ffn_in", "w_pq_in", "o_cur", "mixed", "f_sum", "f_mean", "f_root", "h_row", "h_turned", "h2T", "q_up", "q_kept", "routed", "s_kept",
            "sk_turned", "skT_ready", "f_centered", "f_exped", "s_free", "o_up", "dve_past", "pool_past",
            "e_u", "e_v", "act_past", "dotted", "gelu", "wts", "diag", "v_done", "acc_done", "y_read", "y_ready", "y_out",
            "m_part", "m_turned", "m_diag", "m_all", "centered", "s_exped", "weighted", "o_scaled", "o_turned", "o_kept", "v_lat")}

        landed = [sem(f"landed{r}") for r in range(NRING)]
        freed = [sem(f"freed{r}") for r in range(NRING)]

        block = ctx.enter_context(nc.Block())

        def hold(eng, s, value):
            eng.wait_ge(s, value)

        def meet(eng, k):
            eng.drain()
            eng.sem_inc(all_here, 1)
            eng.wait_ge(all_here, 5 * k)

        def load_index_keys(eng, queue, g0, g1):
            with eng.Fori(0, NB // 2) as bb:
                for e in range(2):
                    hold(eng, S["kidx_free"], 2 * bb + e + 1)
                    for g in range(g0, g1):
                        page = eng.value_load(pages[0:1, ds((2 * bb + e) * NPG + g, 1)], min_val=0, max_val=NPHYS - 1)
                        eng.dma_start(kidx[e][:, g, :], a["cache_a_kidx"][ds(page, 1)].rearrange("a p c -> (a p) c")).then_inc(S[f"kidx_{queue}{e}"], 16)

        def pool_ready(eng, k=1):
            eng.wait_ge(S["pool_step"], k)

        def s_bank(q):
            return ps[2 + q] if q < 2 else ps[5][:, 256:256 + NTOK]

        SOFT = 2

        UNITS = [(blk, c) for blk in range(4) for c in range(2)]
        NCONST = 16 * (13 + HA + KVA)

        @block.sync
        def _(sp):
            sp.dma_start(ident[:], a["c_ident"]).then_inc(ident_in, 16)
            sp.dma_start(xall[:, 0:4, :], a["x_prompt"].rearrange("a (t p) d -> p (a t) d", p=P)).then_inc(x_in, 16)
            for half in range(2):
                sp.dma_start(xall[NTOK * half:NTOK * (half + 1), 4, :], a["x_sample"].rearrange("a t d -> (a t) d")).then_inc(x_in, 16)
            sp.dma_start(g_mix_col[:], a["g_norm_mix"].rearrange("(c p) -> p c", p=P), allow_slow_non_contiguous=True).then_inc(g_mix_in, 16)
            sp.dma_start(g_cq_col[:], a["g_cq"].rearrange("(c p) -> p c", p=P), allow_slow_non_contiguous=True).then_inc(const_in, 16)
            sp.dma_start(rope_a[:], a["c_rope_a"]).then_inc(const_in, 16)
            sp.dma_start(rope_b[:], a["c_rope_b"]).then_inc(const_in, 16)
            sp.dma_start(causal[:], a["c_causal"]).then_inc(const_in, 16)

            sp.dma_start(fold[:], a["c_fold"]).then_inc(const_in, 16)
            sp.dma_start(ones[:], a["c_ones"]).then_inc(const_in, 16)
            sp.dma_start(new_keys[:], a["c_new_keys"]).then_inc(const_in, 16)
            sp.dma_start(new_rows[:], a["c_new_rows"]).then_inc(const_in, 16)
            sp.dma_start(pages[:], a["page_table"].rearrange("(o b) g -> o (b g)", o=1)).then_inc(const_in, 16)

            def row(name, n):
                return a[name].rearrange("(o d) -> o d", o=1).broadcast_to([P, n])

            sp.dma_start(g_kidx[:], row("g_k_idx", DI)).then_inc(const_in, 16)
            sp.dma_start(g_ckv[:], row("g_ckv", DC)).then_inc(const_in, 16)
            sp.dma_start(g_qk[:, 0, :], row("g_q_b", DQK)).then_inc(const_in, 16)
            sp.dma_start(g_qk[:, 1, :], row("g_k_b", DQK)).then_inc(const_in, 16)
            for h in range(HA + KVA):
                sp.dma_start(g_heads[:, h, :], row("g_q_a" if h < HA else "g_k_a", DH)).then_inc(const_in, 16)
            def store(t, dst):
                n = P if dst == "p" else NTOK
                for name, c0, w in (("a_k", OKA, 128), ("a_v", OVA, 128), ("a_kidx", OKI, DI), ("b_ckv", OCKV, DC), ("b_kpe", OKPE, DR)):
                    out = o[f"{dst}_{name}"]
                    rows = out[ds(t * P, P), :] if dst == "p" else out
                    sp.dma_start(rows, cur[0:n, c0:c0 + w]).then_inc(rows_out, 16)

            sp.sem_inc(rows_left, 1)
            with sp.Fori(0, NTILE - 1) as t:
                hold(sp, cur_normed, t + 1)
                store(t, "p")
                sp.wait_ge(rows_out, 16 * 5 * (t + 1))
                sp.sem_inc(rows_left, 1)
            sp.wait_ge(cur_normed, NTILE)
            store(0, "s")
            sp.wait_ge(rows_out, 16 * 5 * NTILE)
            sp.sem_inc(rows_left, 1)
            meet(sp, 1)
            pool_ready(sp)
            load_index_keys(sp, "sp", 0, NPG // 2)
            meet(sp, 2)

            def load_w_out_a():
                for k in range(KVA):
                    rows = a["w_out"][k * G * DH:(k + 1) * G * DH, :].rearrange("(g d) n -> d g n", g=G)
                    sp.dma_start(w_out[k * DH:(k + 1) * DH, 0:G, :], rows).then_inc(S["w_out_a_in"], 16)

            sp.wait_ge(S["scored"], len(UNITS) * G)
            load_w_out_a()
            meet(sp, 3)

            def load_router(again):
                if again:
                    load_w_out_a()
                sp.dma_start(w_out[:, G:, :], a["w_out"][HA * DH:, :].rearrange("(c p) n -> p c n", p=P)).then_inc(S["w_out_b_in"], 16)
                if not again:
                    sp.dma_start(sk[:], a["peer_sub_keys"].rearrange("h p n d -> n (h p) d")).then_inc(S["sk_in"], 16)
                    sp.dma_start(g_ffn[:], row("g_norm_ffn", D)).then_inc(S["g_ffn_in"], 16)
                    sp.dma_start(iota16[:], a["c_iota16"]).then_inc(S["g_ffn_in"], 16)
                sp.dma_start(w_pq[:], a["w_peer_q"].rearrange("(c p) n -> p c n", p=P)).then_inc(S["w_pq_in"], 16)

            load_router(False)
            meet(sp, 4)
            pool_ready(sp, 3)
            with sp.Fori(0, NB) as b:
                ids = [sp.value_load(pages[0:1, ds(b * NPG + g, 1)], min_val=0, max_val=NPHYS - 1) for g in range(NPG)]
                for key, buf, cache, w, new in (("k", k_s, "cache_a_k", P, "s_a_k"), ("pe", pe_s, "cache_b_kpe", DR, "s_b_kpe"),
                                                ("v", v_s, "cache_a_v", P, "s_a_v"), ("c", c_s, "cache_b_ckv", DC, "s_b_ckv")):
                    hold(sp, S[key + "_free"], b + 1)
                    flat = a[cache].rearrange("a p h d -> a p (h d)") if key in "kv" else a[cache]
                    for g in range(NPG):
                        sp.dma_start(buf[:, g, 0:w], flat[ds(ids[g], 1)].rearrange("a p c -> (a p) c")).then_inc(S[key + "_in"], 16)
                    sp.dma_start(buf[0:NT, NPG, 0:w], o[new][ds(b * NT, NT), :]).then_inc(S[key + "_in"], 16)
            meet(sp, 5)
            load_router(True)
            meet(sp, 6)

        @block.gpsimd
        def _(pool):
            meet(pool, 1)
            nc.gpsimd.memset(kidxT[:, NPG, :], 0.0)
            nc.gpsimd.memset(i_row[0:NTOK, PAST:], NEG).then_inc(S["pool_step"], 1)
            load_index_keys(pool, "pool", NPG // 2, NPG)
            meet(pool, 2)
            meet(pool, 3)
            nc.gpsimd.memset(experts[:, NTILE - 1, :], 0).then_inc(S["pool_step"], 1)
            meet(pool, 4)
            for buf in (k_s, v_s, c_s, pe_s):
                nc.gpsimd.memset(buf[:, NPG, :], 0.0)
            nc.gpsimd.memset(q_blk[:], 0.0).then_inc(S["pool_made"], 1)
            pool.wait_ge(S["pool_made"], 1)
            nc.gpsimd.memset(v_s[:, :, P:P + 1], 1.0)
            nc.gpsimd.memset(c_s[:, :, DC:DC + 1], 1.0).then_inc(S["pool_step"], 1)

            def gather(t, cols, eye, width, more=0):
                def weigh(m):
                    if m == 0:
                        hold(pool, S["wts"], t + 1)
                        pool.sem_inc(S["pool_past"], 1)
                    nc.gpsimd.tensor_scalar(diag[:, m // EACH % NDIAG, 0:width], eye, wts[:, m:m + 1], None, ALU.mult).then_inc(S["diag"], 1)

                for k in range(2 * cols):
                    n, r = k % cols, k % NRING
                    if n == 0:
                        hold(pool, S["e_u"] if k == 0 else S["e_v"], t + 1 + (more if k == 0 else 0))
                        pool.sem_inc(S["pool_past"], 1)
                    hold(pool, freed[r], 32 * t + k // NRING + 1)
                    pool.sem_inc(S["pool_past"], 1)
                    table, ids = ("peer_u", e_u) if k < cols else ("peer_v", e_v)
                    pool.indirect_dma_start(ring[:, r, :], None, a[table], bass.IndirectOffsetOnAxis(ap=ids[:, n:n + 1], axis=0)).then_inc(landed[r], 16)
                    if k >= cols + 4 and n % EACH == 0:
                        weigh(n - 4)
                weigh(cols - 4)

            with pool.Fori(0, NTILE - 1) as t:
                gather(t, P, ident[:], P)
            meet(pool, 5)
            meet(pool, 6)
            gather(NTILE - 1, P // 2, fold[:], NTOK, 1)

        @block.scalar
        def _(act):
            for i, (c0, w) in enumerate(group_cols(DIN)):
                act.dma_start(w_in[:, :, c0:c0 + w], a["w_in"][:, c0:c0 + w].rearrange("(c p) n -> p c n", p=P)).then_inc(w_in_in[i], 16)
            act.dma_start(w_uq[:], a["w_uq"].rearrange("(c p) n -> p c n", p=P)).then_inc(weights_in, 16)
            act.dma_start(w_uk[:], a["w_uk"].rearrange("(c p) n -> p c n", p=P)).then_inc(weights_in, 16)
            act.dma_start(w_uv[:], a["w_uv"].rearrange("(c p) n -> p c n", p=P)).then_inc(weights_in, 16)
            act.wait_ge(x_in, 48)

            def x_norm(t):
                nc.scalar.activation(xn[:], xall[:, ds(t, 1), :].rearrange("p a d -> p (a d)"), ACT.Square,
                                     accum_out=stat[:, 0:1]).then_inc(x_sum, 1)
                hold(act, x_mean, t + 1)
                nc.scalar.activation(stat[:, 2:3], stat[:, 1:2], ACT.Sqrt).then_inc(x_root, 1)

            def keep_x(t):
                hold(act, x_turned, t + 1)
                for c in range(KD):
                    last = nc.scalar.activation(xT[:, c, :], ps[c // 4][:, (c % 4) * P:(c % 4 + 1) * P], ACT.Copy,
                                                scale=g_mix_col[:, c:c + 1])
                last.then_inc(xT_ready, 1)

            def keep_projected(t):
                for i, (c0, w) in enumerate(group_cols(DIN)):
                    hold(act, proj_done, 4 * t + i + 1)
                    src, dst = ps[2 + i][:, 0:w], cur[:, c0:c0 + w]
                    if i == 0:
                        src = src.rearrange("p (k g d) -> p k g d", k=KVA, g=G)
                        dst = dst.rearrange("p (g k d) -> p k g d", k=KVA, g=G)
                    last = nc.scalar.activation(dst, src, ACT.Copy)
                last.then_inc(cur_ready, 1)

            def project(t, following):
                cols = ds(t * P, P)
                if following > 0:
                    keep_x(t + 1)
                hold(act, cur_mean, t + 1)
                nc.scalar.activation(stat[:, 16:29], stat[:, 16:29], ACT.Sqrt).then_inc(cur_root, 1)
                if following > 1:
                    x_norm(t + 2)
                hold(act, cur_turned, t + 1)
                for c in range(3):
                    nc.scalar.activation(cqT[:, c, :], ps[1][:, P + c * P:2 * P + c * P], ACT.Copy, scale=g_cq_col[:, c:c + 1])
                nc.scalar.activation(ckvT[:], ps[6][:, 0:2 * P].rearrange("p (c k) -> p c k", c=2), ACT.Copy)
                nc.scalar.activation(qaT[:, :, cols], ps[0][:].rearrange("p (g k) -> p g k", g=G), ACT.Copy)
                nc.scalar.activation(kaT[:, cols], ps[1][:, 0:P], ACT.Copy)
                nc.scalar.activation(kiT[:, cols], ps[6][:, 2 * P:3 * P], ACT.Copy)
                nc.scalar.activation(qiT[:, :, cols], ps[7][:, 0:2 * P].rearrange("p (g k) -> p g k", g=2), ACT.Copy).then_inc(latents_ready, 1)
                nc.scalar.activation(va[:, ds(t, 1), :], cur[:, OVA:OVA + 128].unsqueeze(1), ACT.Copy)
                nc.scalar.activation(wi[:, ds(t, 1), :], cur[:, OWI:OWI + HI].unsqueeze(1), ACT.Copy)
                hold(act, up_done, t + 1)
                qb2 = qb[:].rearrange("p h d -> p (h d)")
                nc.scalar.activation(qb2[:, 0:512], ps[0][:], ACT.Copy)
                nc.scalar.activation(qb2[:, 512:768], ps[1][:, 0:256], ACT.Copy)
                nc.scalar.activation(kb[:, :, 0:DN], ps[6][:].rearrange("p (h d) -> p h d", h=HB), ACT.Copy)
                nc.scalar.activation(vb[:, ds(t, 1), :], ps[7][:].unsqueeze(1), ACT.Copy).then_inc(up_ready, 1)
                hold(act, up_mean, t + 1)
                nc.scalar.activation(stat[:, 32:48], stat[:, 32:48], ACT.Sqrt).then_inc(up_root, 1)
                if following > 0:
                    keep_projected(t + 1)
                hold(act, up_turned, t + 1)
                for i in range(2):
                    nc.scalar.activation(qbT[:, 4 * i:4 * i + 4, cols], ps[i][0:DQK, :].rearrange("p (g k) -> p g k", g=4), ACT.Copy)
                    last = nc.scalar.activation(kbT[:, 4 * i:4 * i + 4, cols], ps[6 + i][0:DQK, :].rearrange("p (g k) -> p g k", g=4), ACT.Copy)
                last.then_inc(tile_kept, 1)

            x_norm(0)
            act.wait_ge(g_mix_in, 16)
            keep_x(0)
            x_norm(1)
            keep_projected(0)
            act.wait_ge(const_in, NCONST)
            with act.Fori(0, NTILE - 2) as t:
                project(t, 2)
            project(NTILE - 2, 1)
            project(NTILE - 1, 0)
            meet(act, 1)
            for i in range(1, 4):
                act.wait_ge(S["idx_summed"], i)
                nk = (i + 1) * P
                for h in range(HI):
                    act.wait_ge(S["idx_scored"], HI * (i - 1) + h + 1)
                    nc.scalar.activation(relus[:, h, 0:nk], ps[h][:, 0:nk], ACT.Relu).then_inc(S["idx_relu"], 1)
            for h in range(HI):
                nc.scalar.activation(qi_s[0:DI, h, :], qiT[64 * (h % 2):64 * (h % 2) + 64, h // 2, SAMP:SAMP + NTOK], ACT.Copy)
            nc.scalar.activation(qa_s[:], qaT[:, :, SAMP:SAMP + NTOK], ACT.Copy)
            nc.scalar.activation(q_pe[0:DR], qbT[DN:DQK, :, SAMP:SAMP + NTOK], ACT.Copy).then_inc(S["qi_ready"], 1)
            act.wait_ge(S["w_bcast"], 1)
            nc.scalar.activation(w_all[:].rearrange("p b (h t) -> p b h t", h=HI), ps[6][:, 0:HI * NTOK].rearrange("p (h b t) -> p b h t", h=HI, b=NB), ACT.Copy).then_inc(S["w_ready"], 1)
            for i in range(2):
                act.wait_ge(S["uk_turned"], i + 1)
                for j in range(2):
                    last = nc.scalar.activation(ukT[0:DN, 2 * j:2 * j + 2, :], ps[j][0:DN, :].rearrange("p (h c) -> p h c", h=2), ACT.Copy)
                last.then_inc(S["uk_ready"], 1)
                act.wait_ge(S["q_lat"], i + 1)
                nc.scalar.activation(qabs[:, :, 4 * i:4 * i + 4, :].rearrange("p c h t -> p h c t"),
                                     ps[2 + i][:].rearrange("p (h c t) -> p h c t", h=4, c=2), ACT.Copy).then_inc(S["qabs_ready"], 1)
            pool_ready(act)
            with act.Fori(0, NB // 2) as bb:
                for e in range(2):
                    b = 2 * bb + e
                    hold(act, S["i_turned"], b + 1)
                    nc.scalar.activation(kidxT[0:DI, NPG, 0:NT], kiT[0:DI, ds(SAMP + b * NT, NT)], ACT.Copy)
                    for q in range(4):
                        last = nc.scalar.activation(kidxT[0:DI, 4 * q:4 * q + 4, :], ps[q][0:DI, :].rearrange("p (g k) -> p g k", g=4), ACT.Copy)
                    last.then_inc(S["i_ready"], 1)
            meet(act, 2)
            def attention(first, q_src, k_scale, o_chunk):
                with act.Fori(0, 4) as g:
                    n0 = first + 8 * g
                    hold(act, S["head_done"], g + 1 + first // 8)
                    q_src(g).then_inc(S["head_q"], 1)

                    def out(u):
                        blk, c = UNITS[u]
                        hold(act, S["inverted"], n0 + u + 1)
                        hold(act, S["attended"], n0 + u + 1)
                        nc.scalar.activation(o_pair[:, blk, c * 64:c * 64 + 64], ps[4 + u % 2][:, 0:64], ACT.Copy,
                                             scale=stat[:, 50 + u % 2:51 + u % 2]).then_inc(S["normed_o"], 1)

                    for u, (blk, c) in enumerate(UNITS):
                        nk = (blk + 1) * P
                        hold(act, S["biased"], n0 + u + 1)
                        nc.scalar.activation(p_cur[:, u % 2, 0:nk], s_cur[:, u % 2, 0:nk], ACT.Exp, scale=k_scale,
                                             bias=stat[:, 2 + u % 2:3 + u % 2],
                                             accum_out=stat[:, 4 + u % 2:5 + u % 2]).then_inc(S["exped"], 1)
                        if u:
                            out(u - 1)
                        hold(act, S["p_turned"], n0 + u + 1)
                        nc.scalar.activation(pT[:, u % 2, 0:nk], ps[2 + u % 2][:, 0:nk], ACT.Copy).then_inc(S["pT_ready"], 1)
                    out(7)
                    hold(act, S["pair_turned"], g + 1 + first // 8)
                    nc.scalar.activation(oT[:, ds(g + o_chunk, 1), 0:SEQ], ps[6][:].unsqueeze(1), ACT.Copy).then_inc(S["pair_kept"], 1)

            attention(0, lambda g: nc.scalar.activation(q_cur[:, 0:1, :], qaT[:, ds(g, 1), 0:SEQ], ACT.Copy), DH ** -0.5, 0)
            attention(32, lambda g: nc.scalar.activation(q_cur[0:DQK, :, :], qbT[:, ds(2 * g, 2), 0:SEQ], ACT.Copy), DQK ** -0.5, G)
            act.wait_ge(S["i_back"], 1)
            for q, (g0, n) in enumerate(group_cols(NPG + 1, 8)):
                nc.scalar.activation(sel_s[:, g0:g0 + n, :], ps[q][:, 0:n * NTOK].rearrange("p (g t) -> p g t", g=n), ACT.Copy)
            meet(act, 3)
            def route(t, packed=False, first=False):
                nc.scalar.activation(o_cur[:], oT[:, :, ds(t * P, P)], ACT.Copy).then_inc(S["o_cur"], 1)
                if first:
                    act.wait_ge(S["sk_turned"], 1)
                    for j in range(2):
                        last = nc.scalar.activation(skT[:, 4 * j:4 * j + 4, :], ps[6 + j][:].rearrange("p (h n) -> p h n", h=4), ACT.Copy)
                    last.then_inc(S["skT_ready"], 1)
                hold(act, S["mixed"], 2 * t + 2)
                x1 = xall[:, ds(t, 1), :].rearrange("p a d -> p (a d)")
                nc.scalar.activation(h_row[:], x1, ACT.Square, accum_out=stat[:, 40:41]).then_inc(S["f_sum"], 1)
                hold(act, S["f_mean"], t + 1)
                nc.scalar.activation(stat[:, 42:43], stat[:, 41:42], ACT.Sqrt).then_inc(S["f_root"], 1)
                hold(act, S["h_row"], t + 1)
                act.sem_inc(S["act_past"], 1)
                nc.scalar.activation(oT[:, :, ds(t * P, P)], h_row[:].rearrange("p (c k) -> p c k", c=KD), ACT.Copy)
                hold(act, S["h_turned"], t + 1)
                for j in range(2):
                    last = nc.scalar.activation(h2T[:, 4 * j:4 * j + 4, :], ps[2 + j][:].rearrange("p (c k) -> p c k", c=4), ACT.Copy)
                last.then_inc(S["h2T"], 1)
                for j in range(2):
                    hold(act, S["q_up"], 2 * t + j + 1)
                    nc.scalar.activation(qpT[:, 4 * j:4 * j + 4, :], ps[4 + j][:].rearrange("p (h k) -> p h k", h=4), ACT.Copy).then_inc(S["q_kept"], 1)
                hold(act, S["s_free"], t + 1)
                for j, bank in enumerate((0, 1, 6, 7)):
                    hold(act, S["routed"], 4 * t + j + 1)
                    rows, x = slice(0, P), 4 * j
                    if packed:
                        rows, x = slice(NTOK * (j // 2), NTOK * (j // 2) + NTOK), 4 * (j % 2)
                    nc.scalar.activation(s_pk[rows, x:x + 4, :], ps[bank][rows, :].rearrange("p (h k) -> p h k", h=4), ACT.Copy).then_inc(S["s_kept"], 1)

            def gate(t, heads=PH):
                hold(act, S["f_centered"], t + 1)
                nc.scalar.activation(cv[:, 0:heads], cv[:, 0:heads], ACT.Exp).then_inc(S["f_exped"], 1)

            route(0, first=True)
            with act.Fori(0, NTILE - 2) as t:
                route(t + 1)
                gate(t)
            gate(NTILE - 2)
            meet(act, 4)
            pool_ready(act, 3)

            def softmax(n, scale):
                hold(act, S["centered"], n)
                nc.scalar.activation(s_s[:], s_s[:], ACT.Exp, scale=scale).then_inc(S["s_exped"], 1)

            def sample_attention(b):
                cols = ds(SAMP + b * NT, NT)
                hold(act, S["q_free"], b + 1)
                for c in range(KVA):
                    r = slice(64 * c, 64 * c + 64)
                    last = nc.scalar.activation(q_blk[r, 32 * c:32 * c + 32].rearrange("p (g t) -> p g t", g=G), qa_s[r, :, ds(b * NT, NT)], ACT.Copy)
                last.then_inc(S["q_blk"], 1)
                for q, (g0, n) in enumerate(group_cols(NPG + 1, 4)):
                    hold(act, S["k_turned"], 5 * b + q + 1)
                    nc.scalar.activation(kT_s[:, q % 2, 0:n, :], ps[q % 2][:, 0:n * P].rearrange("p (g k) -> p g k", g=n), ACT.Copy).then_inc(S["k_ready"], 1)
                softmax(SOFT * b + 1, DH ** -0.5)
                hold(act, S["o_turned"], SOFT * b + 1)
                for c in range(KVA):
                    r = slice(64 * c, 64 * c + 64)
                    last = nc.scalar.activation(oT[r, 0:G, cols], ps[5][r, 32 * c:32 * c + 32].rearrange("p (g t) -> p g t", g=G), ACT.Copy)
                last.then_inc(S["o_kept"], 1)
                for g in range(NPG + 1):
                    n = (NPG + 1) * b + g + 1
                    hold(act, S["c_turned"], n)
                    nc.scalar.activation(cT_s[:, g % 2, 0:2, :], ps[g % 2][:, 0:2 * P].rearrange("p (c k) -> p c k", c=2), ACT.Copy)
                    nc.scalar.activation(cT_s[0:DR, g % 2, 2, :], ps[g % 2][0:DR, 2 * P:3 * P], ACT.Copy).then_inc(S["c_ready"], 1)
                    hold(act, S["nope"], n)
                    if g >= 2:
                        hold(act, S["reduced"], n - 2)
                    nc.scalar.activation(sq_s[:, g % 2, :], ps[4][:], ACT.Square).then_inc(S["squared"], 1)
                hold(act, S["b_mean"], b + 1)
                nc.scalar.activation(norm_s[:], norm_s[:], ACT.Sqrt).then_inc(S["b_root"], 1)
                softmax(SOFT * b + 2, DQK ** -0.5)
                hold(act, S["o_turned"], SOFT * b + 2)
                nc.scalar.activation(olT[:, :, :, ds(b * NT, NT)].rearrange("p c h t -> p (c h) t"),
                                     ps[5][:, 0:2 * NTOK].rearrange("p (x t) -> p x t", t=NT), ACT.Copy).then_inc(S["o_kept"], 1)

            def gelu(t, cols):
                hold(act, S["dotted"], t + 1)
                nc.scalar.activation(acts[:, 0:cols], acts[:, 0:cols], ACT.Gelu_apprx_tanh).then_inc(S["gelu"], 1)

            act.sem_inc(S["y_out"], 16)
            with act.Fori(0, NTILE - 1) as t:
                sample_attention(2 * t)
                gelu(t, P)
                sample_attention(2 * t + 1)
                hold(act, S["y_ready"], t + 1)
                act.dma_start(o["p_y"][ds(t * P, P), :], y_cur[:]).then_inc(S["y_out"], 16)
            act.wait_ge(S["v_lat"], 1)
            for j in range(4):
                for c in range(2):
                    r = slice(64 * c, 64 * c + 64)
                    nc.scalar.activation(oT[r, G + j, SAMP:SAMP + NTOK], ps[0][r, P * j + 64 * c:P * j + 64 * c + 64], ACT.Copy)
            act.drain()
            nc.scalar.activation(oT[:, :, SAMP + NTOK:SAMP + 2 * NTOK], oT[:, :, SAMP:SAMP + NTOK], ACT.Copy)
            act.wait_ge(S["y_out"], 16 * NTILE)
            meet(act, 5)
            route(NTILE - 1, packed=True)
            gate(NTILE - 1, PH // 2)
            meet(act, 6)
            gelu(NTILE - 1, P // 2)
            act.wait_ge(S["y_ready"], NTILE)
            act.dma_start(o["s_y"], y_cur[0:NTOK]).then_inc(S["y_out"], 16)
            act.wait_ge(S["y_out"], 16 * (NTILE + 1))

        @block.vector
        def _(dve):
            v = nc.vector

            def settle():
                dve.drain()

            def rope(x, n, half, tab, t):
                shape = [P, n, half]
                cos = tab[:, 0, ds(t, 1), :].broadcast_to(shape)
                sin = tab[:, 1, ds(t, 1), :].broadcast_to(shape)
                x1, x2 = x[:, :, 0:half], x[:, :, half:2 * half]
                tmp = [rt[:, i, 0:n * half].rearrange("p (n k) -> p n k", n=n) for i in range(4)]
                v.tensor_tensor(tmp[0], x1, cos, ALU.mult)
                v.tensor_tensor(tmp[1], x2, sin, ALU.mult)
                v.tensor_tensor(tmp[2], x2, cos, ALU.mult)
                v.tensor_tensor(tmp[3], x1, sin, ALU.mult)
                settle()
                v.tensor_tensor(x1, tmp[0], tmp[1], ALU.subtract)
                v.tensor_tensor(x2, tmp[2], tmp[3], ALU.add)
                settle()

            dve.wait_ge(x_in, 48)
            def x_norm(t):
                hold(dve, x_sum, t + 1)
                v.tensor_scalar(stat[:, 1:2], stat[:, 0:1], 1.0 / D, EPS, ALU.mult, ALU.add).then_inc(x_mean, 1)
                hold(dve, x_root, t + 1)
                v.reciprocal(stat[:, 3:4], stat[:, 2:3])
                settle()
                v.tensor_scalar(xn[:], xall[:, ds(t, 1), :].rearrange("p a d -> p (a d)"), stat[:, 3:4], None,
                                ALU.mult).then_inc(x_normed, 1)

            def project(t, following):
                hold(dve, tile_kept, t + 1)
                hold(dve, cur_ready, t + 1)
                at = 0
                squares = []
                for c0, w in ((0, 640), (OKI, DI), (OCQ, DCQ), (OCKV, DC)):
                    squares.append(cur_sq[:, at:at + w])
                    v.tensor_tensor(squares[-1], cur[:, c0:c0 + w], cur[:, c0:c0 + w], ALU.mult)
                    at += w
                settle()
                v.tensor_reduce(stat[:, 16:26], squares[0].rearrange("p (h d) -> p h d", d=DH), AX, ALU.add)
                for i in range(3):
                    v.tensor_reduce(stat[:, 26 + i:27 + i], squares[1 + i], AX, ALU.add)
                settle()
                v.tensor_scalar(stat[:, 16:27], stat[:, 16:27], 1.0 / DH, EPS, ALU.mult, ALU.add)
                v.tensor_scalar(stat[:, 27:28], stat[:, 27:28], 1.0 / DCQ, EPS, ALU.mult, ALU.add)
                v.tensor_scalar(stat[:, 28:29], stat[:, 28:29], 1.0 / DC, EPS, ALU.mult, ALU.add).then_inc(cur_mean, 1)
                hold(dve, cur_root, t + 1)
                v.reciprocal(stat[:, 16:29], stat[:, 16:29])
                settle()
                heads = cur[:, 0:640].rearrange("p (h d) -> p h d", d=DH)
                v.tensor_tensor(heads, heads, stat[:, 16:26].unsqueeze(2).broadcast_to([P, 10, DH]), ALU.mult)
                v.tensor_scalar(cur[:, OCQ:OCQ + DCQ], cur[:, OCQ:OCQ + DCQ], stat[:, 27:28], None, ALU.mult)
                ki, ckv = cur[:, OKI:OKI + DI], cur[:, OCKV:OCKV + DC]
                v.scalar_tensor_tensor(ki, ki, stat[:, 26:27], g_kidx[:], ALU.mult, ALU.mult)
                v.scalar_tensor_tensor(ckv, ckv, stat[:, 28:29], g_ckv[:], ALU.mult, ALU.mult)
                settle()
                v.tensor_tensor(heads, heads, g_heads[:], ALU.mult)
                settle()
                rope(heads, 10, 8, rope_a, t)
                rope(cur[:, OQI:OQI + 320].rearrange("p (h d) -> p h d", d=DI), 5, 8, rope_a, t)
                rope(cur[:, OKPE:OKPE + DR].unsqueeze(1), 1, 16, rope_b, t)
                v.tensor_copy(ki2[:].rearrange("p (a d) -> p a d", a=2), cur[:, OKI:OKI + DI].unsqueeze(1).broadcast_to([P, 2, DI]))
                v.tensor_copy(kb[:, :, DN:DQK], cur[:, OKPE:OKPE + DR].unsqueeze(1).broadcast_to([P, HB, DR])).then_inc(cur_normed, 1)
                if following > 1:
                    x_norm(t + 2)
                hold(dve, up_ready, t + 1)
                rope(qb[:, :, DN:DQK], HB, 16, rope_b, t)
                hold(dve, rows_left, t + 2)
                s8 = up_sq[:, 0:768].rearrange("p (h d) -> p h d", d=DQK)
                s8b = up_sq[:, 768:1536].rearrange("p (h d) -> p h d", d=DQK)
                v.tensor_tensor(s8, qb[:], qb[:], ALU.mult)
                v.tensor_tensor(s8b, kb[:], kb[:], ALU.mult)
                settle()
                v.tensor_reduce(stat[:, 32:48], up_sq[:].rearrange("p (h d) -> p h d", d=DQK), AX, ALU.add)
                settle()
                v.tensor_scalar(stat[:, 32:48], stat[:, 32:48], 1.0 / DQK, EPS, ALU.mult, ALU.add).then_inc(up_mean, 1)
                hold(dve, up_root, t + 1)
                v.reciprocal(stat[:, 32:48], stat[:, 32:48])
                settle()
                v.tensor_tensor(kb[:], kb[:], stat[:, 40:48].unsqueeze(2).broadcast_to([P, HB, DQK]), ALU.mult)
                v.tensor_tensor(qb[:], qb[:], stat[:, 32:40].unsqueeze(2).broadcast_to([P, HB, DQK]), ALU.mult)
                settle()
                v.tensor_tensor(qb[:], qb[:], g_qk[:, 0:1, :].broadcast_to([P, HB, DQK]), ALU.mult).then_inc(up_normed, 1)

            x_norm(0)
            hold(dve, x_turned, 1)
            x_norm(1)
            dve.wait_ge(const_in, NCONST)
            v.tensor_tensor(g_qk[:, 0, :], g_qk[:, 0, :], g_qk[:, 1, :], ALU.mult).then_inc(tile_kept, 1)
            with dve.Fori(0, NTILE - 2) as t:
                project(t, 2)
            project(NTILE - 2, 1)
            project(NTILE - 1, 0)
            meet(dve, 1)
            for h in range(HI):
                last = v.tensor_scalar(w_diag[0:NTOK, h, :], ident[0:NTOK, 0:NTOK], wi[0:NTOK, 4, h:h + 1], (HI * DI) ** -0.5, ALU.mult, ALU.mult)
            last.then_inc(S["w_diag"], 1)
            dve.sem_inc(S["idx_summed"], 1)
            rows = [sel[:, i - 1, 0:(i + 1) * P] for i in range(1, 4)]
            seen = [causal[:, 384 - i * P:384 - i * P + (i + 1) * P] for i in range(1, 4)]
            for i in range(1, 4):
                for h in range(HI):
                    dve.wait_ge(S["idx_relu"], HI * (i - 1) + h + 1)
                    v.scalar_tensor_tensor(rows[i - 1], relus[:, h, 0:(i + 1) * P], wi[:, i, h:h + 1], rows[i - 1] if h else seen[i - 1], ALU.mult, ALU.add)
                    settle()
                dve.sem_inc(S["idx_summed"], 1)
            assert KTOP_P // 8 == 2 * NB

            def choose_round():
                for i, row in enumerate(rows):
                    v.max(stat[:, 8 + 8 * i:16 + 8 * i], row)
                settle()
                for i, row in enumerate(rows):
                    v.match_replace(row, stat[:, 8 + 8 * i:16 + 8 * i], row, TAKEN)
                settle()

            dve.wait_ge(S["w_ready"], 1)
            dve.sem_inc(S["i_free"], 1)
            with dve.Fori(0, NB) as b:
                choose_round()
                hold(dve, S["i_scored"], b + 1)
                w = w_all[:, ds(b, 1), :]
                for bank, g0, n in ((4, 0, NPG), (5, NPG, 1)):
                    v.scalar_tensor_tensor(w_relu[:, g0:g0 + n, :], ps[bank][:, 0:n * 32].rearrange("p (g x) -> p g x", g=n),
                                           0.0, w.broadcast_to([P, n, HI * NT]), ALU.max, ALU.mult)
                settle()
                dve.sem_inc(S["i_free"], 1)
                v.tensor_reduce(i_all[:, :, ds(b * NT, NT)], w_relu[:].rearrange("p g (h t) -> p g t h", h=HI), AX, ALU.add)
                choose_round()
            dve.sem_inc(S["i_summed"], 1)
            for row in rows:
                v.tensor_scalar(row, row, TAKEN, -NEG, ALU.is_equal, ALU.mult)
            settle()
            for row, mask in zip(rows, seen):
                v.scalar_tensor_tensor(row, row, NEG, mask, ALU.add, ALU.add)
            dve.wait_ge(S["i_rows"], 1)
            pool_ready(dve)
            for q in range(4):
                v.tensor_copy(i_row[0:NTOK, 512 * q:512 * q + 512], ps[q][0:NTOK, :])
            v.tensor_tensor(i_row[0:NTOK, PAST:PAST + NT], ps[5][0:NTOK, 0:NT], new_rows[:], ALU.add)
            settle()
            meet(dve, 2)
            dve.sem_inc(S["head_done"], 1)

            scores = i_row[0:NTOK, 0:PAST + NT]
            assert KTOP_S // 8 * 2 == 8 * len(UNITS)

            def choose(u):
                if u % 2 == 0:
                    v.max(stat[0:NTOK, 24:32], scores)
                else:
                    v.match_replace(scores, stat[0:NTOK, 24:32], scores, TAKEN)
                settle()

            def attention(first, scale, mask):
                with dve.Fori(0, 4) as g:
                    n0 = first + 8 * g

                    def invert(u):
                        hold(dve, S["exped"], n0 + u + 1)
                        v.reciprocal(stat[:, 50 + u % 2:51 + u % 2], stat[:, 4 + u % 2:5 + u % 2]).then_inc(S["inverted"], 1)

                    for u, (blk, c) in enumerate(UNITS):
                        nk = (blk + 1) * P
                        hold(dve, S["scored"], n0 + u + 1)
                        v.tensor_tensor(s_cur[:, u % 2, 0:nk], ps[u % 2][:, 0:nk], mask(blk, nk), ALU.add)
                        settle()
                        v.tensor_reduce(stat[:, 7:8], s_cur[:, u % 2, 0:nk], AX, ALU.max)
                        settle()
                        v.tensor_scalar(stat[:, 2 + u % 2:3 + u % 2], stat[:, 7:8], -scale, None, ALU.mult).then_inc(S["biased"], 1)
                        choose(u)
                        if u:
                            invert(u - 1)
                    invert(7)

            attention(0, DH ** -0.5, lambda blk, nk: sel[:, blk - 1, 0:nk] if blk else causal[:, 384:384 + nk])
            attention(32, DQK ** -0.5, lambda blk, nk: causal[:, 384 - blk * P:384 - blk * P + nk])
            v.tensor_scalar(scores, scores, TAKEN, -NEG, ALU.is_equal, ALU.mult)
            settle()
            v.tensor_scalar(scores, scores, NEG, None, ALU.add)
            settle()
            v.tensor_tensor(i_row[0:NTOK, PAST:PAST + NT], i_row[0:NTOK, PAST:PAST + NT], new_rows[:], ALU.add).then_inc(S["i_chosen"], 1)
            meet(dve, 3)
            dve.wait_ge(S["g_ffn_in"], 32)
            pool_ready(dve, 2)
            dve.sem_inc(S["s_free"], 1)

            def mix(t):
                for j in range(2):
                    hold(dve, S["o_up"], 2 * t + j + 1)
                    x1 = xall[:, ds(t, 1), 512 * j:512 * j + 512].rearrange("p a d -> p (a d)")
                    v.tensor_tensor(x1, x1, ps[j][:], ALU.add).then_inc(S["mixed"], 1)
                yield
                hold(dve, S["f_sum"], t + 1)
                v.tensor_scalar(stat[:, 41:42], stat[:, 40:41], 1.0 / D, EPS, ALU.mult, ALU.add).then_inc(S["f_mean"], 1)
                yield
                hold(dve, S["f_root"], t + 1)
                v.reciprocal(stat[:, 43:44], stat[:, 42:43])
                settle()
                v.scalar_tensor_tensor(h_row[:], xall[:, ds(t, 1), :].rearrange("p a d -> p (a d)"), stat[:, 43:44], g_ffn[:],
                                       ALU.mult, ALU.mult).then_inc(S["h_row"], 1)
                yield

            def choose_experts(t, others, heads=PH):
                hold(dve, S["s_kept"], 4 * t + 4)
                dve.sem_inc(S["dve_past"], 1)

                def top16(values, indices, scores, n, others=iter(())):
                    for x in range(n):
                        v.max(values(x)[:, 0:8], scores(x))
                    settle()
                    for x in range(n):
                        v.max_index(indices(x)[:, 0:8], values(x)[:, 0:8], scores(x))
                    settle()
                    for x in range(n):
                        v.match_replace(scores(x), values(x)[:, 0:8], scores(x), TAKEN)
                    settle()
                    next(others, None)
                    for x in range(n):
                        v.max(values(x)[:, 8:16], scores(x))
                    settle()
                    next(others, None)
                    for x in range(n):
                        v.max_index(indices(x)[:, 8:16], values(x)[:, 8:16], scores(x))
                    settle()
                    next(others, None)

                at = [(4 * (x // 8) + x % 4, x // 4 % 2) for x in range(2 * heads)]
                top16(lambda x: sv[:, at[x][0], at[x][1], :], lambda x: si[:, at[x][0], at[x][1], :], lambda x: s_pk[:, x, :], 2 * heads, others)
                dve.sem_inc(S["s_free"], 1)
                v.tensor_tensor(cand[:, 0:heads].rearrange("p h (i j) -> p h i j", i=TK), sv[:, 0:heads, 0, :].unsqueeze(3).broadcast_to([P, heads, TK, TK]),
                                sv[:, 0:heads, 1, :].unsqueeze(2).broadcast_to([P, heads, TK, TK]), ALU.add)
                v.tensor_copy(sif[:, 0:heads], si[:, 0:heads])
                settle()
                top16(lambda x: cv[:, x, :], lambda x: ci[:, x, :], lambda x: cand[:, x, :], heads)
                v.tensor_scalar(ci2[:, 0:heads], ci[:, 0:heads], TK - 1, None, ALU.bitwise_and)
                v.tensor_scalar(ci[:, 0:heads], ci[:, 0:heads], 4, None, ALU.logical_shift_right)
                settle()
                v.tensor_copy(cif[:, 0, 0:heads], ci[:, 0:heads])
                v.tensor_copy(cif[:, 1, 0:heads], ci2[:, 0:heads])
                settle()
                for half in range(2):
                    place = cif[:, half, 0:heads].rearrange("p h k -> p (h k)").unsqueeze(2).broadcast_to([P, heads * TK, TK])
                    v.tensor_tensor(hot[:, 0:heads * TK], place, iota16[:].unsqueeze(1).broadcast_to([P, heads * TK, TK]), ALU.is_equal)
                    settle()
                    hot4 = hot[:, 0:heads * TK].rearrange("p (h k) j -> p h k j", h=heads)
                    v.tensor_tensor(hot4, hot4, sif[:, 0:heads, half, :].unsqueeze(2).broadcast_to([P, heads, TK, TK]), ALU.mult)
                    settle()
                    v.tensor_reduce(esel[:, half, 0:heads], hot4, AX, ALU.add)
                    settle()
                v.scalar_tensor_tensor(experts[:, ds(t, 1), 0:heads * TK], esel[:, 0:1, 0:heads].rearrange("p a h k -> p a (h k)"), float(NK),
                                       esel[:, 1:2, 0:heads].rearrange("p a h k -> p a (h k)"), ALU.mult, ALU.add)
                v.tensor_copy(m_gate[:, 0:heads], cv[:, 0:heads, 0:1].rearrange("p h a -> p (h a)"))
                settle()
                v.tensor_tensor(cv[:, 0:heads], cv[:, 0:heads], m_gate[:, 0:heads].unsqueeze(2).broadcast_to([P, heads, TK]), ALU.subtract).then_inc(S["f_centered"], 1)
                hold(dve, S["f_exped"], t + 1)
                v.tensor_reduce(m_gate[:, 0:heads], cv[:, 0:heads], AX, ALU.add)
                settle()
                v.reciprocal(m_gate[:, 0:heads], m_gate[:, 0:heads])
                settle()
                v.tensor_tensor(gates[:, ds(t, 1), 0:heads * TK].rearrange("p a (h k) -> p (a h) k", h=heads), cv[:, 0:heads], m_gate[:, 0:heads].unsqueeze(2).broadcast_to([P, heads, TK]), ALU.mult)
                settle()

            def all_of(steps):
                for _ in steps:
                    pass

            all_of(mix(0))
            with dve.Fori(0, NTILE - 2) as t:
                choose_experts(t, mix(t + 1))
            choose_experts(NTILE - 2, iter(()))
            meet(dve, 4)
            pool_ready(dve, 3)

            def softmax(n, width, went, f):
                v.tensor_reduce(m_s[:], s_s[:].rearrange("p g c -> p c g"), AX, ALU.max).then_inc(S["m_part"], 1)
                went(f + 0.030)
                hold(dve, S["m_turned"], n)
                v.tensor_reduce(stat[0:NTOK, 20:21], ps[5][0:NTOK, 0:P], AX, ALU.max)
                settle()
                v.tensor_scalar(m_diag[0:NTOK, :], ident[0:NTOK, 0:NTOK], stat[0:NTOK, 20:21], None, ALU.mult).then_inc(S["m_diag"], 1)
                went(f + 0.060)
                hold(dve, S["m_all"], n)
                v.tensor_tensor(s_s[:], s_s[:], ps[5][:, P:P + NTOK].unsqueeze(1).broadcast_to([P, NPG + 1, NTOK]), ALU.subtract).then_inc(S["centered"], 1)
                went(f + 0.090)
                hold(dve, S["weighted"], n)
                v.reciprocal(stat[0:NTOK, 21:22], ps[4][0:NTOK, width:width + 1])
                settle()
                v.tensor_scalar(o_s[0:NTOK, 0:width], ps[4][0:NTOK, 0:width], stat[0:NTOK, 21:22], None, ALU.mult).then_inc(S["o_scaled"], 1)
                settle()

            def sample_attention(b, went):
                went(0.12)
                hold(dve, S["a_scored"], b + 1)
                for q, (g0, n) in enumerate(group_cols(NPG + 1, 8)):
                    m = sel_s[:, g0:g0 + n, ds(b * NT, NT)].unsqueeze(2).broadcast_to([P, n, HA, NT])
                    v.tensor_tensor(s_s[:, g0:g0 + n, :].rearrange("p g (h t) -> p g h t", h=HA),
                                    s_bank(q)[:, 0:n * NTOK].rearrange("p (g h t) -> p g h t", g=n, h=HA), m, ALU.add)
                settle()
                softmax(SOFT * b + 1, P, went, 0.12)
                hold(dve, S["pe_in"], 16 * (NPG + 1) * (b + 1))
                v.tensor_tensor(pe_sq[:], pe_s[:], pe_s[:], ALU.mult)
                settle()
                v.tensor_reduce(pe_norm[:], pe_sq[:], AX, ALU.add)
                for g in range(NPG + 1):
                    went(0.22 + 0.63 * (g + 0.7) / NPG)
                    hold(dve, S["squared"], (NPG + 1) * b + g + 1)
                    v.tensor_reduce(norm_s[:, g, :], sq_s[:, g % 2, :].rearrange("p (h d) -> p h d", h=HB), AX, ALU.add).then_inc(S["reduced"], 1)
                settle()
                v.tensor_tensor(norm_s[:], norm_s[:], pe_norm[:].unsqueeze(2).broadcast_to([P, NPG + 1, HB]), ALU.add)
                settle()
                v.tensor_scalar(norm_s[:], norm_s[:], 1.0 / DQK, EPS, ALU.mult, ALU.add).then_inc(S["b_mean"], 1)
                went(0.88)
                hold(dve, S["b_root"], b + 1)
                v.reciprocal(norm_s[:], norm_s[:])
                settle()
                hold(dve, S["b_scored"], b + 1)
                for q, (g0, n) in enumerate(group_cols(NPG + 1, 8)):
                    v.tensor_tensor(s_s[:, g0:g0 + n, :].rearrange("p g (h t) -> p g h t", h=HB),
                                    s_bank(q)[:, 0:n * NTOK].rearrange("p (g h t) -> p g h t", g=n, h=HB),
                                    norm_s[:, g0:g0 + n, :].unsqueeze(3).broadcast_to([P, n, HB, NT]), ALU.mult)
                settle()
                last = s_s[:, NPG, :].rearrange("p (h t) -> p h t", h=HB)
                v.tensor_tensor(last, last, new_keys[:].unsqueeze(1).broadcast_to([P, HB, NT]), ALU.add)
                settle()
                softmax(SOFT * b + 2, DC, went, 0.88)

            def dots(t, n0, n1):
                for n in range(n0, n1):
                    r = n % NRING
                    hold(dve, landed[r], 16 * (32 * t + n // NRING + 1))
                    v.scalar_tensor_tensor(ring[:, r, :], ring[:, r, :], 1.0, h_cur[:], ALU.mult, ALU.mult,
                                           accum_out=acts[:, n:n + 1]).then_inc(freed[r], 1)

            def sums(t, cols, m0, m1):
                for m in range(m0, m1):
                    if m % EACH == 0:
                        continue
                    r = m % NRING
                    hold(dve, landed[r], 16 * (32 * t + (cols + m) // NRING + 1))
                    if m == 1:
                        v.tensor_scalar(acc[:], ring[:, r, :], wts[:, m:m + 1], None, ALU.mult).then_inc(freed[r], 1)
                    else:
                        v.scalar_tensor_tensor(acc[:], ring[:, r, :], wts[:, m:m + 1], acc[:], ALU.mult, ALU.add).then_inc(freed[r], 1)
                    settle()

            def in_parts(work, cols):
                done = [0]

                def went(f):
                    upto = min(cols, int(cols * f) // 2 * 2)
                    if upto > done[0]:
                        work(done[0], upto)
                        done[0] = upto
                return went

            def weights(t, cols):
                settle()
                dve.sem_inc(S["dotted"], 1)
                hold(dve, S["gelu"], t + 1)

            for r in range(NRING):
                dve.sem_inc(freed[r], 1)
            dve.sem_inc(S["y_read"], 1)
            v.tensor_copy(e_u[:], experts[:, 0, :]).then_inc(S["e_u"], 1)
            with dve.Fori(0, NTILE - 1) as t:
                v.tensor_copy(h_cur[:].rearrange("p (c k) -> p c k", c=KD), oT[:, :, ds(t * P, P)])
                v.tensor_copy(e_v[:], experts[:, ds(t, 1), :].rearrange("p a k -> p (a k)")).then_inc(S["e_v"], 1)
                settle()
                went = in_parts(lambda n0, n1: dots(t, n0, n1), P)
                sample_attention(2 * t, went)
                went(1)
                weights(t, P)
                v.tensor_tensor(wts[:], acts[:], gates[:, ds(t, 1), :].rearrange("p a k -> p (a k)"), ALU.mult).then_inc(S["wts"], 1)
                v.tensor_copy(e_u[:], experts[:, ds(t + 1, 1), :].rearrange("p a k -> p (a k)")).then_inc(S["e_u"], 1)
                settle()
                went = in_parts(lambda m0, m1: sums(t, P, m0, m1), P)
                sample_attention(2 * t + 1, went)
                went(1)
                hold(dve, S["y_out"], 16 * (t + 1))
                v.tensor_tensor(y_cur[:], acc[:], xall[:, ds(t, 1), :].rearrange("p a d -> p (a d)"), ALU.add)
                settle()
                hold(dve, S["v_done"], t + 1)
                for j in range(2):
                    last = v.tensor_tensor(y_cur[:, 512 * j:512 * j + 512], y_cur[:, 512 * j:512 * j + 512], ps[6 + j][:], ALU.add)
                last.then_inc(S["y_ready"], 1)
                settle()
                dve.sem_inc(S["y_read"], 1)
            meet(dve, 5)
            all_of(mix(NTILE - 1))
            choose_experts(NTILE - 1, iter(()), PH // 2)
            meet(dve, 6)
            t, cols = NTILE - 1, P // 2
            v.tensor_copy(h_cur[:].rearrange("p (c k) -> p c k", c=KD), oT[:, :, t * P:(t + 1) * P])
            for ids, name in ((e_u, "e_u"), (e_v, "e_v")):
                v.tensor_copy(ids[:, 0:cols], experts[:, t, 0:cols]).then_inc(S[name], 1)
            settle()
            dots(t, 0, cols)
            weights(t, cols)
            v.tensor_tensor(wts[:, 0:cols], acts[:, 0:cols], gates[:, t, 0:cols], ALU.mult).then_inc(S["wts"], 1)
            settle()
            sums(t, cols, 0, cols)
            dve.sem_inc(S["acc_done"], 1)
            dve.wait_ge(S["v_done"], NTILE)
            for j in range(2):
                last = v.tensor_tensor(y_cur[0:NTOK, 512 * j:512 * j + 512], xall[0:NTOK, t, 512 * j:512 * j + 512], ps[6 + j][0:NTOK, :], ALU.add)
            last.then_inc(S["y_ready"], 1)

        @block.tensor
        def _(pe):
            te = nc.tensor
            pe.wait_ge(ident_in, 16)
            def turn_x(t):
                hold(pe, x_normed, t + 1)
                for c in range(KD):
                    last = te.transpose(ps[c // 4][:, (c % 4) * P:(c % 4 + 1) * P], xn[:, c * P:(c + 1) * P], ident[:])
                last.then_inc(x_turned, 1)

            def project_groups(i0, i1):
                for i, (c0, w) in list(enumerate(group_cols(DIN)))[i0:i1]:
                    for c in range(KD):
                        last = te.matmul(ps[2 + i][:, 0:w], xT[:, c, :], w_in[:, c, c0:c0 + w], start=(c == 0), stop=(c == KD - 1))
                    last.then_inc(proj_done, 1)

            def project(t, following):
                if following > 0:
                    hold(pe, tile_kept, t + 1)
                    turn_x(t + 1)
                    hold(pe, xT_ready, t + 2)
                    hold(pe, cur_ready, t + 1)
                    project_groups(0, 2)
                hold(pe, cur_normed, t + 1)
                for g in range(G):
                    te.transpose(ps[0][:, g * P:(g + 1) * P], cur[:, g * P:(g + 1) * P], ident[:])
                te.transpose(ps[1][:, 0:P], cur[:, OKA:OKA + P], ident[:])
                for c in range(3):
                    te.transpose(ps[1][:, (c + 1) * P:(c + 2) * P], cur[:, OCQ + c * P:OCQ + (c + 1) * P], ident[:])
                for c in range(2):
                    te.transpose(ps[6][:, c * P:(c + 1) * P], cur[:, OCKV + c * P:OCKV + (c + 1) * P], ident[:])
                te.transpose(ps[6][:, 2 * P:3 * P], ki2[:], ident[:])
                for c in range(2):
                    last = te.transpose(ps[7][:, c * P:(c + 1) * P], cur[:, OQI + c * P:OQI + (c + 1) * P], ident[:])
                last.then_inc(cur_turned, 1)
                hold(pe, latents_ready, t + 1)
                for c in range(3):
                    te.matmul(ps[0][:], cqT[:, c, :], w_uq[:, c, 0:512], start=(c == 0), stop=(c == 2))
                for c in range(3):
                    te.matmul(ps[1][:, 0:256], cqT[:, c, :], w_uq[:, c, 512:768], start=(c == 0), stop=(c == 2))
                for c in range(2):
                    te.matmul(ps[6][:], ckvT[:, c, :], w_uk[:, c, :], start=(c == 0), stop=(c == 1))
                for c in range(2):
                    last = te.matmul(ps[7][:], ckvT[:, c, :], w_uv[:, c, :], start=(c == 0), stop=(c == 1))
                last.then_inc(up_done, 1)
                if following > 0:
                    project_groups(2, 4)
                hold(pe, up_normed, t + 1)
                for h in range(HB):
                    te.transpose(ps[h // 4][0:DQK, (h % 4) * P:(h % 4 + 1) * P], qb[:, h, :], ident[:])
                for h in range(HB):
                    last = te.transpose(ps[6 + h // 4][0:DQK, (h % 4) * P:(h % 4 + 1) * P], kb[:, h, :], ident[:])
                last.then_inc(up_turned, 1)

            turn_x(0)
            pe.wait_ge(xT_ready, 1)
            for i in range(4):
                pe.wait_ge(w_in_in[i], 16)
                project_groups(i, i + 1)
            pe.wait_ge(weights_in, 48)
            with pe.Fori(0, NTILE - 2) as t:
                project(t, 2)
            project(NTILE - 2, 1)
            project(NTILE - 1, 0)
            meet(pe, 1)
            for i in range(1, 4):
                for h in range(HI):
                    if i > 1:
                        pe.wait_ge(S["idx_relu"], HI * (i - 2) + h + 1)
                    b = slice(64 * (h % 2), 64 * (h % 2) + 64)
                    te.matmul(ps[h][:, 0:(i + 1) * P], qiT[b, h // 2, i * P:(i + 1) * P], kiT[b, 0:(i + 1) * P], start=True, stop=True).then_inc(S["idx_scored"], 1)
            pe.wait_ge(S["idx_relu"], HI * 3)
            pe.wait_ge(S["w_diag"], 1)
            te.matmul(ps[6][:, 0:HI * NTOK], ones[0:NTOK, :], w_diag[0:NTOK].rearrange("p h t -> p (h t)"), start=True, stop=True).then_inc(S["w_bcast"], 1)
            for i in range(2):
                for h in range(4):
                    for c in range(2):
                        last = te.transpose(ps[h // 2][0:DN, (h % 2) * DC + c * P:(h % 2) * DC + (c + 1) * P], w_uk[:, c, (4 * i + h) * DN:(4 * i + h + 1) * DN], ident[:])
                last.then_inc(S["uk_turned"], 1)
                pe.wait_ge(S["uk_ready"], i + 1)
                for h in range(4):
                    for c in range(2):
                        last = te.matmul(ps[2 + i][:, (2 * h + c) * NTOK:(2 * h + c + 1) * NTOK], ukT[0:DN, h, c * P:(c + 1) * P],
                                         qbT[0:DN, 4 * i + h, SAMP:SAMP + NTOK], start=True, stop=True)
                last.then_inc(S["q_lat"], 1)
            pe.wait_ge(S["qabs_ready"], 2)
            pe.wait_ge(S["qi_ready"], 1)
            pe.sem_inc(S["kidx_free"], 2)
            with pe.Fori(0, NB // 2) as bb:
                for e in range(2):
                    b = 2 * bb + e
                    for queue in ("sp", "pool"):
                        hold(pe, S[f"kidx_{queue}{e}"], 16 * NPG // 2 * (bb + 1))
                        pe.sem_inc(S["pe_past"], 1)
                    for g in range(NPG):
                        last = te.transpose(ps[g // 4][0:DI, (g % 4) * P:(g % 4 + 1) * P], kidx[e][:, g, :], ident[:])
                    last.then_inc(S["i_turned"], 1)
                    hold(pe, S["i_ready"], b + 1)
                    pe.sem_inc(S["kidx_free"], 1)
                    hold(pe, S["i_free"], b + 1)
                    q = qi_s[0:DI, :, ds(b * NT, NT)]
                    for g in range(NPG + 1):
                        dst = (ps[4][:, g * 32:g * 32 + 32] if g < NPG else ps[5][:, 0:32]).rearrange("p (h t) -> p h t", h=HI)
                        last = te.matmul(dst, kidxT[0:DI, g, :], q, start=True, stop=True)
                    last.then_inc(S["i_scored"], 1)
            pe.wait_ge(S["i_summed"], 1)
            for g in range(NPG + 1):
                dst = ps[g // 4][0:NTOK, (g % 4) * P:(g % 4 + 1) * P] if g < NPG else ps[5][0:NTOK, 0:P]
                last = te.transpose(dst, i_all[:, g, :], ident[:])
            last.then_inc(S["i_rows"], 1)
            meet(pe, 2)
            def attention(first, scores, values):
                with pe.Fori(0, 4) as g:
                    n0 = first + 8 * g

                    def score(u):
                        scores(g, u, *UNITS[u]).then_inc(S["scored"], 1)

                    hold(pe, S["head_q"], g + 1 + first // 8)
                    score(0)
                    score(1)
                    for u, (blk, c) in enumerate(UNITS):
                        hold(pe, S["exped"], n0 + u + 1)
                        for k in range(blk + 1):
                            last = te.transpose(ps[2 + u % 2][:, k * P:(k + 1) * P], p_cur[:, u % 2, k * P:(k + 1) * P], ident[:])
                        last.then_inc(S["p_turned"], 1)
                        if u < 6:
                            score(u + 2)
                        elif u == 6:
                            pe.sem_inc(S["head_done"], 1)
                        hold(pe, S["pT_ready"], n0 + u + 1)
                        for k in range(blk + 1):
                            last = te.matmul(ps[4 + u % 2][:, 0:64], pT[:, u % 2, k * P:(k + 1) * P], values(g, c, k), start=(k == 0), stop=(k == blk))
                        last.then_inc(S["attended"], 1)
                    hold(pe, S["normed_o"], n0 + 8)
                    for blk in range(4):
                        last = te.transpose(ps[6][:, blk * P:(blk + 1) * P], o_pair[:, blk, :], ident[:])
                    last.then_inc(S["pair_turned"], 1)

            def scores_a(g, u, blk, c):
                b = slice(64 * c, 64 * c + 64)
                return te.matmul(ps[u % 2][:, 0:(blk + 1) * P], q_cur[b, 0, blk * P:(blk + 1) * P], kaT[b, 0:(blk + 1) * P], start=True, stop=True)

            def scores_b(g, u, blk, c):
                keys = kbT[:, ds(2 * g + c, 1), 0:(blk + 1) * P].rearrange("p a b -> p (a b)")
                return te.matmul(ps[u % 2][:, 0:(blk + 1) * P], q_cur[0:DQK, c, blk * P:(blk + 1) * P], keys, start=True, stop=True)

            attention(0, scores_a, lambda g, c, k: va[:, k, c * DH:(c + 1) * DH])
            attention(32, scores_b, lambda g, c, k: vb[:, k, ds((2 * g + c) * DV, DV)])
            pe.wait_ge(S["i_chosen"], 1)
            for g in range(NPG + 1):
                last = te.transpose(ps[g // 8][:, (g % 8) * NTOK:(g % 8 + 1) * NTOK], i_row[0:NTOK, g * P:(g + 1) * P], ident[0:NTOK, 0:NTOK])
            last.then_inc(S["i_back"], 1)
            meet(pe, 3)
            def route(t, load, first=False):
                hold(pe, S["o_cur"], t + 1)
                pe.wait_ge(S["w_out_a_in"], 32 * load)
                for c in range(KD):
                    if c == G:
                        pe.wait_ge(S["w_out_b_in"], 16 * load)
                    for j in range(2):
                        last = te.matmul(ps[j][:], o_cur[:, c, :], w_out[:, c, 512 * j:512 * j + 512], start=(c == 0), stop=(c == KD - 1))
                        if c == KD - 1:
                            last.then_inc(S["o_up"], 1)
                if first:
                    pe.wait_ge(S["sk_in"], 16)
                    for h in range(PH):
                        last = te.transpose(ps[6 + h // 4][:, (h % 4) * P:(h % 4 + 1) * P], sk[:, 2 * h:2 * h + 2, :].rearrange("p a d -> p (a d)"), ident[:])
                    last.then_inc(S["sk_turned"], 1)
                hold(pe, S["h_row"], t + 1)
                for c in range(KD):
                    last = te.transpose(ps[2 + c // 4][:, (c % 4) * P:(c % 4 + 1) * P], h_row[:, c * P:(c + 1) * P], ident[:])
                last.then_inc(S["h_turned"], 1)
                hold(pe, S["h2T"], t + 1)
                pe.wait_ge(S["w_pq_in"], 16 * load)
                for h in range(PH):
                    for c in range(KD):
                        last = te.matmul(ps[4 + h // 4][:, (h % 4) * P:(h % 4 + 1) * P], w_pq[:, c, h * P:(h + 1) * P], h2T[:, c, :], start=(c == 0), stop=(c == KD - 1))
                    if h % 4 == 3:
                        last.then_inc(S["q_up"], 1)
                pe.wait_ge(S["skT_ready"], 1)
                for j, bank in enumerate((0, 1, 6, 7)):
                    if j % 2 == 0:
                        hold(pe, S["q_kept"], 2 * t + j // 2 + 1)
                    for x in range(4):
                        h, half = 4 * (j // 2) + x, j % 2
                        r = slice(64 * half, 64 * half + 64)
                        last = te.matmul(ps[bank][:, x * P:(x + 1) * P], qpT[r, h, :], skT[r, h, :], start=True, stop=True)
                    last.then_inc(S["routed"], 1)

            route(0, 1, first=True)
            with pe.Fori(0, NTILE - 2) as t:
                route(t + 1, 1)
            meet(pe, 4)
            pool_ready(pe, 3)

            def softmax(n, values, width, chunks, free, went, f):
                went(f + 0.025)
                hold(pe, S["m_part"], n)
                pe.sem_inc(S["pe_past"], 1)
                te.transpose(ps[5][0:NTOK, 0:P], m_s[:], ident[:]).then_inc(S["m_turned"], 1)
                went(f + 0.050)
                hold(pe, S["m_diag"], n)
                te.matmul(ps[5][:, P:P + NTOK], ones[0:NTOK, :], m_diag[0:NTOK, :], start=True, stop=True).then_inc(S["m_all"], 1)
                went(f + 0.075)
                hold(pe, S["s_exped"], n)
                for g in range(NPG + 1):
                    last = te.matmul(ps[4][0:NTOK, 0:width + 1], s_s[:, g, :], values[:, g, :], start=(g == 0), stop=(g == NPG))
                last.then_inc(S["weighted"], 1)
                went(f + 0.100)
                hold(pe, S["o_scaled"], n)
                pe.sem_inc(S[free], 1)
                for c in range(chunks):
                    last = te.transpose(ps[5][:, c * NTOK:(c + 1) * NTOK], o_s[0:NTOK, c * P:(c + 1) * P], ident[0:NTOK, 0:NTOK])
                last.then_inc(S["o_turned"], 1)
                hold(pe, S["o_kept"], n)

            def sample_attention(b, went):
                def s_dst(g):
                    return s_bank(g // 8)[:, g % 8 * NTOK:(g % 8 + 1) * NTOK]

                hold(pe, S["k_in"], 16 * (NPG + 1) * (b + 1))
                hold(pe, S["q_blk"], b + 1)
                for q, (g0, n) in enumerate(group_cols(NPG + 1, 4)):
                    for g in range(n):
                        last = te.transpose(ps[q % 2][:, g * P:(g + 1) * P], k_s[:, g0 + g, :], ident[:])
                    last.then_inc(S["k_turned"], 1)
                    went(0.12 * (q + 1) / 5)
                    hold(pe, S["k_ready"], 5 * b + q + 1)
                    for g in range(g0, g0 + n):
                        last = te.matmul(s_dst(g), kT_s[:, q % 2, g - g0, :], q_blk[:], start=True, stop=True)
                last.then_inc(S["a_scored"], 1)
                pe.sem_inc(S["k_free"], 1)
                hold(pe, S["v_in"], 16 * (NPG + 1) * (b + 1))
                softmax(SOFT * b + 1, v_s, P, 1, "v_free", went, 0.12)
                pe.sem_inc(S["q_free"], 1)
                hold(pe, S["c_in"], 16 * (NPG + 1) * (b + 1))
                hold(pe, S["pe_in"], 16 * (NPG + 1) * (b + 1))

                def turn(g):
                    bank = ps[g % 2]
                    te.transpose(bank[:, 0:P], c_s[:, g, 0:P], ident[:])
                    te.transpose(bank[:, P:2 * P], c_s[:, g, P:2 * P], ident[:])
                    te.transpose(bank[0:DR, 2 * P:3 * P], pe_s[:, g, :], ident[:]).then_inc(S["c_turned"], 1)

                turn(0)
                for g in range(NPG + 1):
                    n = (NPG + 1) * b + g + 1
                    if g < NPG:
                        if g >= 1:
                            hold(pe, S["c_ready"], n - 1)
                        turn(g + 1)
                    went(0.22 + 0.63 * g / NPG)
                    hold(pe, S["c_ready"], n)
                    dst = s_dst(g)
                    cols = ds(b * NT, NT)
                    dst = dst.rearrange("p (h t) -> p h t", h=HB)
                    te.matmul(dst, cT_s[:, g % 2, 0, :], qabs[:, 0, :, cols], start=True, stop=False)
                    te.matmul(dst, cT_s[:, g % 2, 1, :], qabs[:, 1, :, cols], start=False, stop=False)
                    te.matmul(dst, cT_s[0:DR, g % 2, 2, :], q_pe[0:DR, :, ds(b * NT, NT)], start=False, stop=True)
                    if g >= 1:
                        hold(pe, S["squared"], n - 1)
                    bank = ps[4]
                    for c in range(2):
                        last = te.matmul(bank[:], cT_s[:, g % 2, c, :], w_uk[:, c, :], start=(c == 0), stop=(c == 1))
                    last.then_inc(S["nope"], 1)
                pe.sem_inc(S["b_scored"], 1)
                pe.sem_inc(S["pe_free"], 1)
                softmax(SOFT * b + 2, c_s, DC, 2, "c_free", went, 0.88)

            def sums(t, cols, width, m0, m1):
                for m in range(-(-m0 // EACH) * EACH, m1, EACH):
                    r = m % NRING
                    if m == 0:
                        hold(pe, S["y_read"], t + 1)
                    hold(pe, S["diag"], P // EACH * t + m // EACH + 1)
                    hold(pe, landed[r], 16 * (32 * t + (cols + m) // NRING + 1))
                    for j in range(2):
                        last = te.matmul(ps[6 + j][0:width, :], diag[:, m // EACH % NDIAG, 0:width], ring[:, r, 512 * j:512 * j + 512],
                                         start=(m == 0), stop=(m == cols - EACH and width == P), skip_group_check=True)
                    last.then_inc(freed[r], 1)

            def in_parts(work, cols):
                done = [0]

                def went(f):
                    upto = min(cols, int(cols * f) // 2 * 2)
                    if upto > done[0]:
                        work(done[0], upto)
                        done[0] = upto
                return went

            for name in ("k_free", "v_free", "c_free", "pe_free", "q_free"):
                pe.sem_inc(S[name], 1)
            with pe.Fori(0, NTILE - 1) as t:
                sample_attention(2 * t, lambda f: None)
                went = in_parts(lambda m0, m1: sums(t, P, P, m0, m1), P)
                sample_attention(2 * t + 1, went)
                went(1)
                pe.drain()
                pe.sem_inc(S["v_done"], 1)
            for j in range(4):
                for c in range(2):
                    last = te.matmul(ps[0][:, j * P:(j + 1) * P], w_uv[:, c, j * P:(j + 1) * P], olT[:, c, 2 * j:2 * j + 2, :].rearrange("p h t -> p (h t)"), start=(c == 0), stop=(c == 1))
            last.then_inc(S["v_lat"], 1)
            meet(pe, 5)
            route(NTILE - 1, 2)
            meet(pe, 6)
            t, cols = NTILE - 1, P // 2
            sums(t, cols, NTOK, 0, cols)
            pe.wait_ge(S["acc_done"], 1)
            for j in range(2):
                last = te.matmul(ps[6 + j][0:NTOK, :], fold[:], acc[:, 512 * j:512 * j + 512], start=False, stop=True, skip_group_check=True)
            last.then_inc(S["v_done"], 1)


_INS = ["x_prompt", "x_sample", "cache_a_k", "cache_a_v", "cache_a_kidx", "cache_b_ckv", "cache_b_kpe", "page_table",
        "g_norm_mix", "w_in", "g_q_a", "g_k_a", "g_k_idx", "g_cq", "w_uq", "g_ckv", "w_uk", "w_uv", "g_q_b", "g_k_b",
        "w_out", "g_norm_ffn", "w_peer_q", "peer_sub_keys", "peer_u", "peer_v"]
_OUTS = [("p_y", (SEQ, D)), ("s_y", (NTOK, D)),
         ("p_a_k", (SEQ, 128)), ("p_a_v", (SEQ, 128)), ("p_a_kidx", (SEQ, DI)), ("p_b_ckv", (SEQ, DC)), ("p_b_kpe", (SEQ, DR)),
         ("s_a_k", (NTOK, 128)), ("s_a_v", (NTOK, 128)), ("s_a_kidx", (NTOK, DI)), ("s_b_ckv", (NTOK, DC)), ("s_b_kpe", (NTOK, DR))]
_SHAPES = [(1, SEQ, D), (NB, NT, D), (1, SEQ, KVA, DH), (1, SEQ, KVA, DH), (1, SEQ, DI), (1, SEQ, DC), (1, SEQ, DR),
           (NB, NT, KVA, DH), (NB, NT, KVA, DH), (NB, NT, DI), (NB, NT, DC), (NB, NT, DR)]


def shape_constants():
    import numpy as np

    f = np.float32
    pos = np.zeros((NTILE, P), f)
    pos[:NTILE - 1] = np.arange(SEQ, dtype=f).reshape(NTILE - 1, P)
    pos[NTILE - 1, :NTOK] = np.tile(PAST + np.arange(NT, dtype=f), NB)

    def rope(n_rot):
        half = n_rot // 2
        inv = (f(THETA) ** (-np.arange(half, dtype=f) * f(2.0) / f(n_rot))).astype(f)
        ang = (pos[:, :, None] * inv[None, None, :]).astype(f)
        tab = np.stack([np.cos(ang), np.sin(ang)]).astype(f)
        return np.ascontiguousarray(tab.transpose(2, 0, 1, 3))

    j = np.arange(SEQ + 384)[None, :] - 384
    causal = np.where(j <= np.arange(P)[:, None], 0.0, NEG).astype(f)
    key = np.arange(P)[:, None]
    new_keys = np.where(key <= np.arange(NT)[None, :], 0.0, NEG).astype(f)
    new_rows = np.where(np.arange(NT)[None, :] <= np.arange(NTOK)[:, None] % NT, 0.0, NEG).astype(f)
    return {"c_fold": np.tile(np.eye(NTOK, dtype=f), (2, 1)), "c_ones": np.ones((P, P), f), "c_new_keys": new_keys, "c_new_rows": new_rows, "c_iota16": np.tile(np.arange(TK, dtype=f), (P, 1)),
            "c_ident": np.eye(P, dtype=f), "c_rope_a": rope(16), "c_rope_b": rope(32), "c_causal": causal}


def kernel(**inputs):
    import numpy as _np
    import concourse.bacc as _bacc
    from concourse import mybir as _mybir
    from concourse.bass_utils import run_bass_kernel_spmd as _run

    nc = _bacc.Bacc("TRN2", target_bir_lowering=False, num_devices=1)
    arrays, aps = {}, {}
    for name in _INS:
        arrays[name] = _np.ascontiguousarray(inputs[name])
    arrays.update(shape_constants())
    for name, x in arrays.items():
        aps[name] = nc.dram_tensor("in_" + name, x.shape, _mybir.dt.from_np(x.dtype), kind="ExternalInput").ap()
    outs = {n: nc.dram_tensor("out_" + n, s, _mybir.dt.float32, kind="ExternalOutput").ap() for n, s in _OUTS}
    program(nc, aps, outs)
    r = _run(nc, [{"in_" + n: x for n, x in arrays.items()}], core_ids=[0]).results[0]
    return tuple(r["out_" + n].reshape(s) for (n, _), s in zip(_OUTS, _SHAPES))
```
